# Optimizing a Trainium2 kernel written in Bass

```python
import jax
import jax.numpy as jnp
from jax import lax
import numpy as np

D_MODEL = 1024
BATCH = 1
SEQ = 512
DEPTH = 2

GRID_W = 64
CTX_LEN = 256
HEAD_DIM = 128
A_Q_HEADS = 4
A_KV_HEADS = 2
B_Q_HEADS = 4
B_KV_HEADS = 2
A_GROUP = A_Q_HEADS // A_KV_HEADS
B_GROUP = B_Q_HEADS // B_KV_HEADS
A_QW = A_Q_HEADS * HEAD_DIM
A_KVW = A_KV_HEADS * HEAD_DIM
B_QW = B_Q_HEADS * HEAD_DIM
B_KVW = B_KV_HEADS * HEAD_DIM
ATTN_SECTIONS = (A_QW, A_KVW, A_KVW, B_QW, B_KVW, B_KVW)
ATTN_IN = A_QW + 2 * A_KVW + B_QW + 2 * B_KVW
ATTN_MIX = A_QW + B_QW
ATTN_SCALE = HEAD_DIM ** -0.5
Q_BLOCK = 128
WINDOW = 128
ROPE_THETA = 10000.0
ROPE_AXIS_DIM = HEAD_DIM // 2
GLA_HEADS = 4
GLA_KEY_DIM = D_MODEL // 2
GLA_VAL_DIM = D_MODEL
GLA_DK = GLA_KEY_DIM // GLA_HEADS
GLA_DV = GLA_VAL_DIM // GLA_HEADS
GLA_IN = 2 * GLA_KEY_DIM + 2 * GLA_VAL_DIM
GLA_GATE_RANK = 16
GLA_GATE_NORM = 16.0
GLA_CHUNK = 64
D_FF = 2816
CONV_W = 3
N_ATTN_LAYERS = (DEPTH + 1) // 2
N_GLA_LAYERS = DEPTH // 2
DEEPNORM_ALPHA = (2 * DEPTH) ** 0.25
DEEPNORM_BETA = (8 * DEPTH) ** -0.25
EPS = 1e-6

kernel_name = 'hybrid_diffusion_trunk'

def layer_norm(x, g, b):
    xf = x.astype(jnp.float32)
    mu = jnp.mean(xf, axis=-1, keepdims=True)
    var = jnp.mean(jnp.square(xf - mu), axis=-1, keepdims=True)
    return ((xf - mu) * lax.rsqrt(var + EPS) * g + b).astype(x.dtype)

def rms_norm(x, g):
    xf = x.astype(jnp.float32)
    return (xf * lax.rsqrt(jnp.mean(jnp.square(xf), axis=-1, keepdims=True) + EPS) * g).astype(x.dtype)

def to_heads(z, n_heads, head_dim):
    b, t, _ = z.shape
    return z.reshape(b, t, n_heads, head_dim).transpose(0, 2, 1, 3)

def from_heads(z):
    b, h, t, d = z.shape
    return z.transpose(0, 2, 1, 3).reshape(b, t, h * d)

def merge_groups(o):
    b, hk, g, t, d = o.shape
    return from_heads(o.reshape(b, hk * g, t, d))

def axial_rope_tables(rows):
    row = jnp.repeat(jnp.arange(rows, dtype=jnp.float32), GRID_W)
    col = jnp.tile(jnp.arange(GRID_W, dtype=jnp.float32), rows)
    inv_freq = jnp.power(ROPE_THETA, -jnp.arange(ROPE_AXIS_DIM // 2, dtype=jnp.float32) * 2.0 / ROPE_AXIS_DIM)
    ang = jnp.concatenate([row[:, None] * inv_freq, col[:, None] * inv_freq], axis=-1)
    return jnp.cos(ang), jnp.sin(ang)

def apply_rope(z, cos, sin):
    zf = z.astype(jnp.float32)
    z1, z2 = zf[..., :HEAD_DIM // 2], zf[..., HEAD_DIM // 2:]
    return jnp.concatenate([z1 * cos - z2 * sin, z1 * sin + z2 * cos], axis=-1).astype(z.dtype)

def scores(q, k):
    return jnp.einsum('bhgqd,bhkd->bhgqk', q, k).astype(jnp.float32) * ATTN_SCALE

def ada_modulation(cond, w, b):
    return jnp.split(jax.nn.silu(cond) @ w + b, 6, axis=-1)

def attn_project(h, w_in, q_norm, k_norm, rope):
    p = h @ w_in
    parts, off = [], 0
    for width in ATTN_SECTIONS:
        parts.append(p[..., off:off + width])
        off += width
    aq, ak, av, bq, bk, bv = parts
    aq = rms_norm(to_heads(aq, A_Q_HEADS, HEAD_DIM), q_norm)
    ak = rms_norm(to_heads(ak, A_KV_HEADS, HEAD_DIM), k_norm)
    av = to_heads(av, A_KV_HEADS, HEAD_DIM)
    bq = to_heads(bq, B_Q_HEADS, HEAD_DIM)
    bk = to_heads(bk, B_KV_HEADS, HEAD_DIM)
    bv = to_heads(bv, B_KV_HEADS, HEAD_DIM)
    if rope is not None:
        cos, sin = rope
        aq, ak, bq, bk = [apply_rope(z, cos, sin) for z in (aq, ak, bq, bk)]
    b, _, t, _ = aq.shape
    aq = aq.reshape(b, A_KV_HEADS, A_GROUP, t, HEAD_DIM)
    bq = bq.reshape(b, B_KV_HEADS, B_GROUP, t, HEAD_DIM)
    return aq, ak, av, bq, bk, bv

def dense_attention(q, k, v):
    p = jax.nn.softmax(scores(q, k), axis=-1)
    return jnp.einsum('bhgqk,bhkd->bhgqd', p.astype(v.dtype), v)

def global_attention_latent(q, k_lat, v_lat, k_ctx, v_ctx):
    b, hk, g, n, d = q.shape
    nb = n // Q_BLOCK
    k_all = jnp.concatenate([k_lat, k_ctx], axis=2)
    v_all = jnp.concatenate([v_lat, v_ctx], axis=2)
    q_blocks = jnp.moveaxis(q.reshape(b, hk, g, nb, Q_BLOCK, d), 3, 0)
    o = lax.map(lambda qb: dense_attention(qb, k_all, v_all), q_blocks)
    return jnp.moveaxis(o, 0, 3).reshape(b, hk, g, n, d)

def window_attention_latent(q, k_lat, v_lat, k_ctx, v_ctx, sink):
    b, hk, g, n, d = q.shape
    nb = n // Q_BLOCK

    def bands(z):
        zp = jnp.pad(z, ((0, 0), (0, 0), (Q_BLOCK, Q_BLOCK), (0, 0))).reshape(b, hk, nb + 2, Q_BLOCK, d)
        return jnp.concatenate([zp[:, :, :-2], zp[:, :, 1:-1], zp[:, :, 2:]], axis=3)

    kb, vb = bands(k_lat), bands(v_lat)
    qb = q.reshape(b, hk, g, nb, Q_BLOCK, d)
    s_band = jnp.einsum('bhgnqd,bhnkd->bhgnqk', qb, kb).astype(jnp.float32) * ATTN_SCALE
    q_pos = jnp.arange(nb)[:, None, None] * Q_BLOCK + jnp.arange(Q_BLOCK)[None, :, None]
    k_pos = jnp.arange(nb)[:, None, None] * Q_BLOCK - Q_BLOCK + jnp.arange(3 * Q_BLOCK)[None, None, :]
    valid = (jnp.abs(k_pos - q_pos) <= WINDOW) & (k_pos >= 0) & (k_pos < n)
    s_band = jnp.where(valid, s_band, -jnp.inf)
    s_ctx = jnp.einsum('bhgnqd,bhcd->bhgnqc', qb, k_ctx).astype(jnp.float32) * ATTN_SCALE
    s_sink = jnp.broadcast_to(sink.astype(jnp.float32).reshape(1, hk, g, 1, 1, 1), s_ctx.shape[:-1] + (1,))
    p = jax.nn.softmax(jnp.concatenate([s_band, s_ctx, s_sink], axis=-1), axis=-1).astype(v_lat.dtype)
    n_band = 3 * Q_BLOCK
    n_ctx = k_ctx.shape[2]
    o = (jnp.einsum('bhgnqk,bhnkd->bhgnqd', p[..., :n_band], vb)
         + jnp.einsum('bhgnqc,bhcd->bhgnqd', p[..., n_band:n_band + n_ctx], v_ctx))
    return o.reshape(b, hk, g, n, d)

def sink_attention_context(q, k, v, sink):
    b, hk, g, t, d = q.shape
    s = scores(q, k)
    s_sink = jnp.broadcast_to(sink.astype(jnp.float32).reshape(1, hk, g, 1, 1), (b, hk, g, t, 1))
    p = jax.nn.softmax(jnp.concatenate([s, s_sink], axis=-1), axis=-1)[..., :-1]
    return jnp.einsum('bhgqk,bhkd->bhgqd', p.astype(v.dtype), v)

def attn_mixer(h_lat, h_ctx, w_in, q_norm, k_norm, sink, w_out, rope, need_ctx):
    aq, ak, av, bq, bk, bv = attn_project(h_lat, w_in, q_norm, k_norm, rope)
    caq, cak, cav, cbq, cbk, cbv = attn_project(h_ctx, w_in, q_norm, k_norm, None)
    o_a = global_attention_latent(aq, ak, av, cak, cav)
    o_b = window_attention_latent(bq, bk, bv, cbk, cbv, sink)
    y_lat = jnp.concatenate([merge_groups(o_a), merge_groups(o_b)], axis=-1) @ w_out
    y_ctx = None
    if need_ctx:
        co_a = dense_attention(caq, cak, cav)
        co_b = sink_attention_context(cbq, cbk, cbv, sink)
        y_ctx = jnp.concatenate([merge_groups(co_a), merge_groups(co_b)], axis=-1) @ w_out
    return y_lat, y_ctx

def gla_project(h, w_in, w_a1, w_a2, b_a):
    b, t, _ = h.shape
    p = h @ w_in
    q = p[..., :GLA_KEY_DIM]
    k = p[..., GLA_KEY_DIM:2 * GLA_KEY_DIM]
    v = p[..., 2 * GLA_KEY_DIM:2 * GLA_KEY_DIM + GLA_VAL_DIM]
    g = p[..., 2 * GLA_KEY_DIM + GLA_VAL_DIM:]
    q = to_heads(q, GLA_HEADS, GLA_DK) * (GLA_DK ** -0.5)
    k = to_heads(k, GLA_HEADS, GLA_DK)
    v = to_heads(v, GLA_HEADS, GLA_DV)
    low = jnp.einsum('btd,zdr->zbtr', h, w_a1)
    logits = jnp.einsum('zbtr,zrk->zbtk', low, w_a2) + b_a[:, None, None, :]
    log_decay = jax.nn.log_sigmoid(logits.astype(jnp.float32)) / GLA_GATE_NORM
    log_decay = log_decay.reshape(2, b, t, GLA_HEADS, GLA_DK).transpose(0, 1, 3, 2, 4)
    return q, k, v, g, log_decay

def gla_chunk_scan(q, k, v, log_decay, s0):
    b, h, t, dk = q.shape
    dv = v.shape[-1]
    nc = t // GLA_CHUNK

    def chunks(z):
        return jnp.moveaxis(z.astype(jnp.float32).reshape(b, h, nc, GLA_CHUNK, z.shape[-1]), 2, 0)

    lower = jnp.tril(jnp.ones((GLA_CHUNK, GLA_CHUNK), dtype=bool))[:, :, None]

    def step(state, inp):
        qc, kc, vc, lc = inp
        cum = jnp.cumsum(lc, axis=2)
        rel = jnp.where(lower, cum[:, :, :, None, :] - cum[:, :, None, :, :], -jnp.inf)
        attn = jnp.einsum('bhtd,bhsd,bhtsd->bhts', qc, kc, jnp.exp(rel))
        last = cum[:, :, -1:, :]
        out = attn @ vc + jnp.einsum('bhtd,bhdv->bhtv', qc * jnp.exp(cum), state)
        state = (jnp.exp(last[:, :, 0, :, None]) * state
                 + jnp.einsum('bhsd,bhsv->bhdv', kc * jnp.exp(last - cum), vc))
        return state, out

    s_fin, out = lax.scan(step, s0.astype(jnp.float32), (chunks(q), chunks(k), chunks(v), chunks(log_decay)))
    out = jnp.moveaxis(out, 0, 2).reshape(b, h, t, dv)
    return out.astype(v.dtype), s_fin

def gla_output(o, g, head_norm, w_out):
    o = from_heads(rms_norm(o, head_norm))
    return (o * jax.nn.silu(g)) @ w_out

def gla_mixer(h_lat, h_ctx, w_in, w_a1, w_a2, b_a, head_norm, w_out, need_ctx):
    flip = lambda z: jnp.flip(z, axis=2)
    q, k, v, g, ld = gla_project(h_lat, w_in, w_a1, w_a2, b_a)
    cq, ck, cv, cg, cld = gla_project(h_ctx, w_in, w_a1, w_a2, b_a)
    s0 = jnp.zeros((q.shape[0], GLA_HEADS, GLA_DK, GLA_DV), jnp.float32)
    co_f, cs_f = gla_chunk_scan(cq, ck, cv, cld[0], s0)
    co_b, cs_b = gla_chunk_scan(flip(cq), flip(ck), flip(cv), flip(cld[1]), s0)
    o_f, _ = gla_chunk_scan(q, k, v, ld[0], cs_f)
    o_b, _ = gla_chunk_scan(flip(q), flip(k), flip(v), flip(ld[1]), cs_b)
    y_lat = gla_output(o_f + flip(o_b), g, head_norm, w_out)
    y_ctx = None
    if need_ctx:
        y_ctx = gla_output(co_f + flip(co_b), cg, head_norm, w_out)
    return y_lat, y_ctx

def conv_ffn(h, w_up, conv_w, conv_b, w_down):
    t = h.shape[1]
    u = h @ w_up
    half = CONV_W // 2
    up = jnp.pad(u, ((0, 0), (half, half), (0, 0)))
    acc = conv_b + conv_w[0] * up[:, 0:t]
    for j in range(1, CONV_W):
        acc = acc + conv_w[j] * up[:, j:j + t]
    gate, val = jnp.split(acc, 2, axis=-1)
    return (jax.nn.silu(gate) * val) @ w_down

def setup_inputs(seed: int = 0) -> dict:
    key = jax.random.key(seed)
    ks = jax.random.split(key, 23)

    def nrm(k, shape, scale):
        return jax.random.normal(k, shape, jnp.float32) * scale

    d, f = D_MODEL, D_FF
    na, ng = N_ATTN_LAYERS, N_GLA_LAYERS
    return {
        'x': nrm(ks[0], (BATCH, SEQ, d), 1.0),
        'c': nrm(ks[1], (BATCH, d), 1.0),
        'ctx': nrm(ks[2], (BATCH, CTX_LEN, d), 1.0),
        'c_ctx': nrm(ks[3], (d,), 1.0),
        'ada_w': nrm(ks[4], (DEPTH, d, 6 * d), 0.5 * d ** -0.5),
        'ada_b': nrm(ks[5], (DEPTH, 6 * d), 0.01),
        'ln_g': 1.0 + nrm(ks[6], (DEPTH, 2, d), 0.02),
        'ln_b': nrm(ks[7], (DEPTH, 2, d), 0.02),
        'ffn_w_up': nrm(ks[8], (DEPTH, d, 2 * f), d ** -0.5),
        'ffn_conv_w': nrm(ks[9], (DEPTH, CONV_W, 2 * f), CONV_W ** -0.5),
        'ffn_conv_b': nrm(ks[10], (DEPTH, 2 * f), 0.01),
        'ffn_w_down': nrm(ks[11], (DEPTH, f, d), DEEPNORM_BETA * f ** -0.5),
        'attn_w_in': nrm(ks[12], (na, d, ATTN_IN), d ** -0.5),
        'attn_q_norm': 1.0 + nrm(ks[13], (na, HEAD_DIM), 0.02),
        'attn_k_norm': 1.0 + nrm(ks[14], (na, HEAD_DIM), 0.02),
        'attn_sink': nrm(ks[15], (na, B_Q_HEADS), 0.5),
        'attn_w_out': nrm(ks[16], (na, ATTN_MIX, d), DEEPNORM_BETA * ATTN_MIX ** -0.5),
        'gla_w_in': nrm(ks[17], (ng, d, GLA_IN), d ** -0.5),
        'gla_w_a1': nrm(ks[18], (ng, 2, d, GLA_GATE_RANK), d ** -0.5),
        'gla_w_a2': nrm(ks[19], (ng, 2, GLA_GATE_RANK, GLA_KEY_DIM), GLA_GATE_RANK ** -0.5),
        'gla_b_a': 1.0 + nrm(ks[20], (ng, 2, GLA_KEY_DIM), 0.5),
        'gla_head_norm': 1.0 + nrm(ks[21], (ng, GLA_DV), 0.02),
        'gla_w_out': nrm(ks[22], (ng, GLA_VAL_DIM, d), DEEPNORM_BETA * GLA_VAL_DIM ** -0.5),
    }

def reference(x, c, ctx, c_ctx, ada_w, ada_b, ln_g, ln_b, ffn_w_up, ffn_conv_w, ffn_conv_b, ffn_w_down,
              attn_w_in, attn_q_norm, attn_k_norm, attn_sink, attn_w_out,
              gla_w_in, gla_w_a1, gla_w_a2, gla_b_a, gla_head_norm, gla_w_out):
    rows = x.shape[1] // GRID_W
    rope = axial_rope_tables(rows)
    h, hc = x, ctx
    for i in range(DEPTH):
        need_ctx = i < DEPTH - 1
        sh1, sc1, g1, sh2, sc2, g2 = [m[:, None, :] for m in ada_modulation(c, ada_w[i], ada_b[i])]
        csh1, csc1, cg1, csh2, csc2, cg2 = ada_modulation(c_ctx, ada_w[i], ada_b[i])
        a_lat = h * (1 + sc1) + sh1
        a_ctx = hc * (1 + csc1) + csh1
        j = i // 2
        if i % 2 == 0:
            y, yc = attn_mixer(a_lat, a_ctx, attn_w_in[j], attn_q_norm[j], attn_k_norm[j], attn_sink[j],
                               attn_w_out[j], rope, need_ctx)
        else:
            y, yc = gla_mixer(a_lat, a_ctx, gla_w_in[j], gla_w_a1[j], gla_w_a2[j], gla_b_a[j],
                              gla_head_norm[j], gla_w_out[j], need_ctx)
        h = layer_norm(DEEPNORM_ALPHA * h + g1 * y, ln_g[i, 0], ln_b[i, 0])
        f = conv_ffn(h * (1 + sc2) + sh2, ffn_w_up[i], ffn_conv_w[i], ffn_conv_b[i], ffn_w_down[i])
        h = layer_norm(DEEPNORM_ALPHA * h + g2 * f, ln_g[i, 1], ln_b[i, 1])
        if need_ctx:
            hc = layer_norm(DEEPNORM_ALPHA * hc + cg1 * yc, ln_g[i, 0], ln_b[i, 0])
            fc = conv_ffn(hc * (1 + csc2) + csh2, ffn_w_up[i], ffn_conv_w[i], ffn_conv_b[i], ffn_w_down[i])
            hc = layer_norm(DEEPNORM_ALPHA * hc + cg2 * fc, ln_g[i, 1], ln_b[i, 1])
    return h


_drawn_inputs = setup_inputs


def setup_inputs(seed=0):
    import zlib

    import numpy as np

    out = dict(_drawn_inputs(seed))
    spreads = {}
    factors = {'ctx': 4.134,
     'c_ctx': 3.07,
     'ada_b': 8.0,
     'ffn_conv_b': 25.443,
     'attn_q_norm': 8.0,
     'attn_k_norm': 8.0,
     'attn_sink': 64.0,
     'gla_w_a1': 3.751,
     'gla_w_a2': 3.864,
     'gla_b_a': 3.005,
     'gla_head_norm': 46.752}
    for name, (base, spread) in spreads.items():
        noise = np.random.default_rng([zlib.crc32(name.encode()), seed]).standard_normal(out[name].shape)
        drawn = base * np.exp(spread * noise) if base else spread * noise
        out[name] = jnp.asarray(drawn.astype(out[name].dtype))
    for name, factor in factors.items():
        out[name] = (out[name] * factor).astype(out[name].dtype)
    return out
```

```python
from contextlib import ExitStack

import concourse.bass as bass
from concourse import mybir

FP32 = mybir.dt.float32
FP32R = mybir.dt.float32r
ALU = mybir.AluOpType
ACT = mybir.ActivationFunctionType
AX = mybir.AxisListType

P = 128
D_MODEL = 1024
KT = D_MODEL // P
LAT = 512
CTX = 256
TOK = LAT + CTX
GRID_W = 64
HEAD_DIM = 128
WINDOW = 128
N_HEADS = 4
N_KV = 2
D_FF = 2816
FT = D_FF // P
FF_GROUPS = (8, 8, 6)
CONV_W = 3
GLA_HEADS = 4
GLA_RANK = 16
GLA_CHUNK = 128
GLA_LEVELS = 7
ATTN_SCALE = HEAD_DIM ** -0.5
ALPHA = 4 ** 0.25
EPS = 1e-6
ROPE_THETA = 10000.0
MASKED = -1e30

ATTN_COLS = [0, 1, 2, 3, 4, 5, 8, 9, 10, 11, 12, 13, 6, 7, 14, 15]
HEAD_OF = {"aq": 0, "ak": 4, "bq": 6, "bk": 10, "av": 12, "bv": 14}
N_ATTN_IN = 16
S_ATTN_OUT = N_ATTN_IN
S_FFN0 = S_ATTN_OUT + KT
N_FFN = 2 * FT + KT * len(FF_GROUPS)
S_GLA = S_FFN0 + N_FFN
N_GLA_ALL = 1 + 4 + 8
N_GLA_LAT = 4 + 8
S_GLA_OUT = S_GLA + N_GLA_ALL + N_GLA_LAT
S_FFN1 = S_GLA_OUT + KT
N_SLABS = S_FFN1 + N_FFN

ADA_TILES = 48
SH1, SC1, G1, SH2, SC2, G2 = range(0, ADA_TILES, KT)

VEC_WIDTHS = [("cond", 2 * KT), ("ada_b", 2 * ADA_TILES), ("ln_g", 4 * KT), ("ln_b", 4 * KT),
              ("conv_w", 2 * CONV_W * 2 * FT), ("conv_b", 2 * 2 * FT), ("q_norm", 1), ("k_norm", 1),
              ("sink", N_HEADS), ("b_a", 2 * GLA_HEADS), ("head_norm", 2), ("eps", 1)]
VEC = {}
_at = 0
for _name, _w in VEC_WIDTHS:
    VEC[_name] = _at
    _at += _w
N_VEC = _at


class Order:

    def __init__(self, engine, sem):
        self.engine, self.sem, self.n, self.extra = engine, sem, 0, 0

    def mark(self, instruction):
        instruction.then_inc(self.sem, 1)
        self.n += 1
        return self.n + self.extra

    def wait(self, value=None):
        self.engine.wait_ge(self.sem, self.n + self.extra if value is None else value)

    def enter(self, i, per):
        self.extra, self.start, self.per = i * per, self.n, per

    def leave(self, count):
        assert self.n - self.start == self.per, (self.n - self.start, self.per)
        self.n, self.extra = self.start + self.per * count, 0


def trunk(nc, x_in, vec_in, slabs_in, ada_in, rope_in, band_in, eye_in, a2_in, level_in, out):
    ctx = ExitStack()
    with ctx:
        top = [(nc.sbuf_base + 31) // 32 * 32]

        def place(name, shape, dtype=FP32, at=None):
            size = 4
            for n in shape:
                size *= n
            where = top[0] if at is None else at
            if at is None:
                top[0] += (size + 31) // 32 * 32
            return nc.alloc_sbuf_tensor_at(name, [P, *shape], dtype, offset=where)

        h_res = place("h_res", [KT, TOK])
        x_at = top[0]
        x_hi = place("x_hi", [KT, TOK], FP32R)
        x_lo = place("x_lo", [KT, TOK], FP32R)
        hid_at = top[0]
        hid_hi = place("hid_hi", [KT, TOK], FP32R)
        hid_lo = place("hid_lo", [KT, TOK], FP32R)
        raw = [place(f"raw{j}", [KT * P]) for j in range(4)]
        w_hi = [place(f"w_hi{j}", [KT * P], FP32R) for j in range(2)]
        w_lo = [place(f"w_lo{j}", [KT * P], FP32R) for j in range(2)]
        ada_at = top[0]
        ada_w = [place(f"ada_w{j}", [2, KT * P]) for j in range(2)]
        vec = place("vec", [N_VEC])
        mods = place("mods", [2, ADA_TILES, 2])
        cond = place("cond", [KT, 2])
        mean_w = place("mean_w", [P])
        ones = place("ones", [P])
        eye = place("eye", [P])
        place("chunk_sums", [4 * GLA_HEADS * 7])
        free_at = top[0]
        assert free_at < nc.sbuf_usable_end

        def scratch(at, *shapes, dtype=FP32):
            got = []
            for name, shape in shapes:
                size = 4
                for n in shape:
                    size *= n
                got.append(nc.alloc_sbuf_tensor_at(name, [P, *shape], dtype, offset=at))
                at += (size + 31) // 32 * 32
            assert at <= nc.sbuf_usable_end, (shapes, at, nc.sbuf_usable_end)
            return got, at

        [qkv], _ = scratch(hid_at, ("qkv", [N_ATTN_IN, TOK]))
        [rope, band, v_tok, row], attn_at = scratch(
            free_at, ("rope", [2, LAT]), ("band", [3 * P]), ("v_tok", [TOK // P, 4 * P]), ("row", [8, 8]))
        [score, probs, probs_t], _ = scratch(
            attn_at, ("score", [5 * P]), ("probs", [2, TOK]), ("probs_t", [2, TOK]))
        [rope_c, rope_s], _ = scratch(attn_at + 2560, ("rope_c", [2, LAT]), ("rope_s", [2, LAT]))
        [square], _ = scratch(ada_at, ("square", [5, TOK]))
        [square_5], _ = scratch(free_at + 5632, ("square_5", [TOK]))
        [norm], _ = scratch(x_at, ("norm", [6, TOK]))
        [sum1, sum2, mean, rstd, tmp, acc_g, acc_v, hid_f, pool_t], _ = scratch(
            free_at, ("sum1", [TOK]), ("sum2", [TOK]), ("mean", [TOK]), ("rstd", [TOK]), ("tmp", [2, TOK]),
            ("acc_g", [TOK]), ("acc_v", [TOK]), ("hid_f", [TOK]), ("pool_t", [2, TOK]))

        [gla_v, cum], _ = scratch(hid_at, ("gla_v", [TOK // P, 8 * P]), ("cum", [2, GLA_HEADS, TOK]))
        [a2, restart], _ = scratch(ada_at, ("a2", [2, GLA_HEADS * P]), ("restart", [TOK]))
        [gla_g], _ = scratch(ada_at, ("gla_g", [KT, LAT]))
        [gla_k, gla_q], gla_at = scratch(free_at, ("gla_k", [GLA_HEADS, TOK]), ("gla_q", [GLA_HEADS, LAT]))
        [low, soft, clipped], _ = scratch(
            gla_at, ("low", [TOK]), ("soft", [2, TOK]), ("clipped", [TOK]))
        [v_turn], _ = scratch(gla_at + 4 * TOK, ("v_turn", [2, TOK]))
        level = nc.alloc_sbuf_tensor_at("level", [P, 2 * GLA_LEVELS, P], mybir.dt.uint8, offset=gla_at)
        [q_in, o_buf, k_out], at = scratch(
            gla_at + 2 * GLA_LEVELS * P, ("q_in", [2, LAT]), ("o_buf", [2, LAT]), ("k_out", [TOK]))
        [k_tok], _ = scratch(gla_at + 2 * GLA_LEVELS * P + 8 * LAT, ("k_tok", [5, P]))
        [level_f], _ = scratch(gla_at + 2 * GLA_LEVELS * P, ("level_f", [2 * GLA_LEVELS, P]))
        [chunk_sum, decay], _ = scratch(top[0] - 448, ("chunk_sum", [2, GLA_HEADS, 6]), ("decay", [2, GLA_HEADS, 6]))
        [o_hi2, o_lo2], at = scratch(x_at, ("o_hi2", [KT, LAT]), ("o_lo2", [KT, LAT]), dtype=FP32R)
        [pairs, fade, both, o_rms], _ = scratch(
            at, ("pairs", [2, LAT]), ("fade", [3, LAT]), ("both", [2, LAT]), ("o_rms", [LAT]))

        pm = [ctx.enter_context(nc.psum_tensor(f"pm{j}", [P, 1024], FP32)) for j in range(4)]

        names = ["split_hi", "split_lo", "slab_done", "psum_free", "ada_done", "mods_done",
                 "vec_in", "x_loaded", "const_in", "cond_done", "ones_done", "x_ready", "hid_ready",
                 "act_seq", "dve_seq", "pool_seq", "out_done",
                 "ssq_done", "qkv_copied", "squared", "normed", "roped", "rope_p", "v_turned", "v_copied",
                 "score_done", "shift_done", "exp_done", "probs_done", "turned", "turn_copied", "pv_done",
                 "pv_copied", "o_hi", "gated", "residual", "summed", "stat_done", "h_ready", "mod_f",
                 "x_hi_done", "centred", "std_done", "lin_done", "silu_done", "acc_free", "hid_split",
                 "a2_in", "level_in", "level_done", "low_done", "logit_done", "abs_done", "log_done", "ld_done", "restart_done",
                 "diff_done", "fade_done", "both_done", "gram_done", "level_used", "q_diff", "q_exp", "q_done",
                 "k_diff", "k_exp", "k_done", "k_turned", "k_copied", "s_prod", "s_done", "decay_done",
                 "o_done", "o_sq", "o_ssq", "o_std", "o_rms", "o_scaled", "o_gated", "o_hi_done", "o_ready",
                 "exp_sink", "mean_out", "var_done", "std2"]
        sem = {n: ctx.enter_context(nc.semaphore(n)) for n in names}
        raw_in = [ctx.enter_context(nc.semaphore(f"raw_in{j}")) for j in range(4)]
        ada_in_sem = [ctx.enter_context(nc.semaphore(f"ada_in{j}")) for j in range(2)]
        block = ctx.enter_context(nc.Block())

        def col(name, k=0, n=1):
            return vec[:, bass.ds(VEC[name] + k, n)]

        HALVES = ((0, LAT), (LAT, TOK))
        LEVELS = 1 + 2 * GLA_LEVELS
        SCAN = ((4, 5, 0, 1, 2), (5, 4, 3, 2, 1))
        STATE = ((3, 0, 1, 2, 3), (0, 3, 2, 1, 0))

        def state(z, c):
            return h_res[:, 4 * z + c, LAT:TOK]

        def state_sum(j):
            return (pm[3][:, 256 * j:256 * (j + 1)] if j < 4 else pm[1][:, 512:768])

        def segments(b, z, h, src=None):
            m = 1 << b
            v = (cum[:, z, h, 0:LAT] if src is None else src).rearrange("p (n t) -> p n t", t=2 * m)
            mid = m - 1 if z == 0 else m
            return v[:, :, 0:m], v[:, :, m:2 * m], v[:, :, mid:mid + 1].to_broadcast([P, LAT // (2 * m), m])

        def chunks(v):
            return v.rearrange("p (n t) -> p n t", t=GLA_CHUNK)

        @block.sync
        def _(sp):
            sp.dma_start(vec[:, :], vec_in).then_inc(sem["vec_in"], 16)

            def ada_load(n):
                if n >= 2:
                    sp.wait_ge(sem["ada_done"], 2 * (n - 1))
                sp.dma_start(ada_w[n % 2][:, :, :].rearrange("p a b -> p (a b)"), ada_in[n]).then_inc(
                    ada_in_sem[n % 2], 16)

            for n in range(8):
                ada_load(n)
                if n == 1:
                    sp.dma_start(h_res[:, :, :], x_in).then_inc(sem["x_loaded"], 16)
                    sp.dma_start(eye[:, :], eye_in).then_inc(sem["const_in"], 16)
                    sp.dma_start(rope[:, :, :], rope_in).then_inc(sem["const_in"], 16)
                    sp.dma_start(band[:, :], band_in).then_inc(sem["const_in"], 16)

            def slab_load(s, slot):
                if not (isinstance(s, int) and s < 4):
                    sp.wait_ge(sem["split_lo"], s - 3)
                sp.dma_start(raw[slot][:, :], slabs_in[s]).then_inc(raw_in[slot], 16)

            for s in range(4):
                slab_load(s, s)
            with sp.Fori(1, 5) as i:
                for u in range(4):
                    slab_load(4 * i + u, u)
            for n in range(8, 24):
                if n == 8:
                    sp.wait_ge(sem["ssq_done"], 6)
                ada_load(n)
            with sp.Fori(5, 7) as i:
                for u in range(4):
                    slab_load(4 * i + u, u)
            for n in range(24, 36):
                ada_load(n)
            with sp.Fori(7, 24) as i:
                for u in range(4):
                    slab_load(4 * i + u, u)
            for n in range(36, 48):
                ada_load(n)
            sp.wait_ge(sem["ada_done"], 96)
            sp.dma_start(a2[0:2 * GLA_RANK, :, :], a2_in).then_inc(sem["a2_in"], 16)
            with sp.Fori(24, 29) as i:
                for u in range(4):
                    slab_load(4 * i + u, u)
            sp.wait_ge(sem["v_copied"], TOK // P + 8)
            sp.dma_start(level_f[:, :, :], level_in).then_inc(sem["level_in"], 16)
            with sp.Fori(29, N_SLABS // 4) as i:
                for u in range(4):
                    slab_load(4 * i + u, u)
            slab_load(N_SLABS - 1, (N_SLABS - 1) % 4)
            sp.wait_ge(sem["h_ready"], 4 * KT)
            sp.dma_start(out, h_res[:, :, 0:LAT]).then_inc(sem["out_done"], 16)
            sp.wait_ge(sem["out_done"], 16)

        @block.tensor
        def _(pe):
            def ada_tiles(first, count):
                for a in range(first, first + count):
                    n, half = a // 2, a % 2
                    if half == 0:
                        pe.wait_ge(ada_in_sem[n % 2], 16 * (n // 2 + 1))
                    for k in range(KT):
                        last = pe.matmul(pm[3][:, 512 + 2 * a:514 + 2 * a], ada_w[n % 2][:, half, k * P:(k + 1) * P],
                                         cond[:, k, :], start=(k == 0), stop=(k == KT - 1))
                    last.then_inc(sem["ada_done"], 1)

            def slab(base, i, u, hi, lo, tokens, tiles=KT, ready=None, value=0):
                s = base + u + i * 4
                slot, out_p = (base + u) % 2, pm[(base + u) % 2]
                pe.wait_ge(sem["split_lo"], s + 1)
                if not (isinstance(s, int) and s < 2):
                    pe.wait_ge(sem["psum_free"], s - 1)
                for k in range(tiles):
                    if ready is not None:
                        pe.wait_ge(ready, value + k + 1)
                    ks = slice(k * P, (k + 1) * P)
                    for w, x in ((w_hi, hi), (w_hi, lo), (w_lo, hi)):
                        for a, b in HALVES if tokens == TOK else HALVES[:1]:
                            last = pe.matmul(out_p[:, a:b], w[slot][:, ks], x[:, k, a:b],
                                             start=(k == 0 and w is w_hi and x is hi),
                                             stop=(k == tiles - 1 and w is w_lo))
                last.then_inc(sem["slab_done"], 1)

            def stats(tokens=TOK):
                for j, part in ((0, sum1), (1, sum2)):
                    for a, b in HALVES if tokens == TOK else HALVES[:1]:
                        last = pe.matmul(pm[j][:, a:b], mean_w[:, :], part[:, a:b], start=True, stop=True)
                last.then_inc(sem["stat_done"], 1)

            pe.wait_ge(sem["cond_done"], 1)
            ada_tiles(0, 16)
            for u in range(4):
                slab(0, 0, u, x_hi, x_lo, TOK, ready=sem["x_ready"] if u == 0 else None)
            with pe.Fori(1, 4) as i:
                for u in range(4):
                    slab(0, i, u, x_hi, x_lo, TOK)

            pe.wait_ge(sem["psum_free"], N_ATTN_IN)
            pe.wait_ge(sem["ones_done"], 2)
            for h in range(6):
                if h >= 3:
                    pe.wait_ge(sem["std_done"], h - 2)
                pe.wait_ge(sem["squared"], h + 1)
                src = square[:, h, :] if h < 5 else square_5[:, :]
                for a, b in HALVES:
                    last = pe.matmul(pm[h % 3][:, a:b], ones[:, :], src[:, a:b], start=True, stop=True)
                last.then_inc(sem["ssq_done"], 1)
            ada_tiles(16, 32)
            pe.wait_ge(sem["const_in"], 48)
            for t in range(TOK // P):
                if t >= 1:
                    pe.wait_ge(sem["v_copied"], t)
                else:
                    pe.wait_ge(sem["std_done"], 6)
                for f in range(4):
                    last = pe.transpose(pm[2][:, f * P:(f + 1) * P],
                                        qkv[:, HEAD_OF["av"] + f, t * P:(t + 1) * P], eye[:, :])
                last.then_inc(sem["v_turned"], 1)

            def scores(n):
                u = UNITS[n]
                if n == 0:
                    pe.wait_ge(sem["roped"], 12)
                    pe.wait_ge(sem["normed"], 6)
                if n >= 2:
                    pe.wait_ge(sem["exp_done"], n - 1)
                q = qkv[:, u["q"], u["q0"]:u["q0"] + P]
                for at, a, b in u["spans"]:
                    last = pe.matmul(pm[n % 2][:, at:at + b - a], q, qkv[:, u["k"], a:b], start=True, stop=True)
                last.then_inc(sem["score_done"], 1)

            def turn(n):
                u = UNITS[n]
                pe.wait_ge(sem["probs_done"], n + 1)
                if n == 0:
                    pe.wait_ge(sem["v_copied"], TOK // P)
                else:
                    pe.wait_ge(sem["turn_copied"], n)
                for j in range(len(u["tiles"])):
                    last = pe.transpose(pm[2][:, j * P:(j + 1) * P], probs[:, n % 2, j * P:(j + 1) * P], eye[:, :])
                last.then_inc(sem["turned"], 1)

            def weigh(n):
                u = UNITS[n]
                pe.wait_ge(sem["turn_copied"], n + 1)
                if n == 0:
                    pe.wait_ge(sem["mods_done"], 2)
                if u["first"] and u["out"] >= 2:
                    pe.wait_ge(sem["pv_copied"], u["out"] - 1)
                at = 512 * (u["out"] % 2) + u["o0"]
                for j, t in enumerate(u["tiles"]):
                    last = pe.matmul(pm[3][:, at:at + P], v_tok[:, t, u["v"] * P:(u["v"] + 1) * P],
                                     probs_t[:, n % 2, j * P:(j + 1) * P], start=(j == 0), stop=(j == len(u["tiles"]) - 1))
                if u["last"]:
                    last.then_inc(sem["pv_done"], 1)

            scores(0)
            for n in range(len(UNITS)):
                if n + 1 < len(UNITS):
                    scores(n + 1)
                if n >= 1:
                    weigh(n - 1)
                turn(n)
            weigh(len(UNITS) - 1)

            pe.wait_ge(sem["pv_copied"], len(OUTS))
            with pe.Fori(0, 2) as i:
                for u in range(4):
                    slab(S_ATTN_OUT, i, u, x_hi, x_lo, TOK)
            pe.wait_ge(sem["summed"], KT)
            pe.wait_ge(sem["psum_free"], S_FFN0)
            stats()
            ada_tiles(ADA_TILES, 24)

            def ffn(base, layer, tokens):
                s = base
                for g, tiles in enumerate(FF_GROUPS):
                    with pe.Fori(0, tiles // 2) as i:
                        for u in range(4):
                            slab(s, i, u, x_hi, x_lo, tokens, ready=sem["x_ready"] if u == 0 and g == 0 else None,
                                 value=(1 + 2 * layer) * KT)
                    s += 2 * tiles
                    with pe.Fori(0, 2) as i:
                        for u in range(4):
                            slab(s, i, u, hid_hi, hid_lo, tokens, tiles, ready=sem["hid_ready"] if u == 0 else None,
                                 value=FT * layer + sum(FF_GROUPS[:g]))
                    s += KT

            ffn(S_FFN0, 0, TOK)
            pe.wait_ge(sem["summed"], 2 * KT)
            pe.wait_ge(sem["psum_free"], S_GLA)
            stats()
            ada_tiles(ADA_TILES + 24, 24)

            def logits(j):
                z, h = j // GLA_HEADS, j % GLA_HEADS
                if j == 0:
                    pe.wait_ge(sem["low_done"], 1)
                    pe.wait_ge(sem["a2_in"], 16)
                    pe.wait_ge(sem["mods_done"], 4)
                if j >= 2:
                    pe.wait_ge(sem["ld_done"], j - 1)
                for a, b in HALVES:
                    last = pe.matmul(pm[2 + j % 2][:, a:b], a2[0:2 * GLA_RANK, z, h * P:(h + 1) * P],
                                     low[0:2 * GLA_RANK, a:b], start=True, stop=True)
                last.then_inc(sem["logit_done"], 1)

            slab(S_GLA, 0, 0, x_hi, x_lo, TOK, ready=sem["x_ready"], value=2 * KT)
            for n in range(GLA_HEADS):
                slab(S_GLA, 0, n + 1, x_hi, x_lo, TOK)
                logits(2 * n)
                logits(2 * n + 1)
            s_v = S_GLA + 1 + GLA_HEADS
            pe.wait_ge(sem["ld_done"], 2 * GLA_HEADS)
            with pe.Fori(0, 2) as i:
                def turn_v(u):
                    pe.wait_ge(sem["psum_free"], s_v + u + 1 + 4 * i)
                    pe.wait_ge(sem["v_copied"], TOK // P + u - 1 + 4 * i)
                    for t in range(TOK // P):
                        last = pe.transpose(pm[2 + u % 2][:, t * P:(t + 1) * P], v_turn[:, u % 2, t * P:(t + 1) * P],
                                            eye[:, :])
                    last.then_inc(sem["v_turned"], 1)

                for u in range(4):
                    slab(s_v, i, u, x_hi, x_lo, TOK)
                    if u >= 1:
                        turn_v(u - 1)
                turn_v(3)
            with pe.Fori(0, 3) as i:
                for u in range(4):
                    slab(S_GLA + N_GLA_ALL, i, u, x_hi, x_lo, LAT)

            pe.wait_ge(sem["psum_free"], S_GLA_OUT)
            pe.wait_ge(sem["v_copied"], TOK // P + 8)
            for h in range(GLA_HEADS):
                for z in range(2):
                    q = 2 * h + z
                    pe.wait_ge(sem["k_done"], q + 1)
                    if q >= 1:
                        pe.wait_ge(sem["k_copied"], q)
                    for j, c in enumerate(SCAN[z]):
                        last = pe.transpose(pm[2][:, j * P:(j + 1) * P], k_out[:, c * P:(c + 1) * P], eye[:, :])
                    last.then_inc(sem["k_turned"], 1)
                    pe.wait_ge(sem["k_copied"], q + 1)
                    if q >= 1:
                        pe.wait_ge(sem["s_done"], 5 * q)
                    if z == 0 and h >= 1:
                        pe.wait_ge(sem["o_scaled"], 2 * h)
                    for j, c in enumerate(SCAN[z]):
                        last = pe.matmul(state_sum(j), k_tok[:, j, :], gla_v[:, c, 2 * h * P:2 * (h + 1) * P],
                                         start=True, stop=True)
                    last.then_inc(sem["s_prod"], 1)
                for lv in range(LEVELS):
                    n = LEVELS * h + lv
                    if n >= 3:
                        pe.wait_ge(sem["level_used"], n - 2)
                    if lv > 0:
                        m = (LEVELS - 1) * h + lv - 1
                        pe.wait_ge(sem["both_done"], m + 1)
                        lhs, rhs = both[:, m % 2, :], both[:, m % 2, :]
                    else:
                        lhs, rhs = gla_k[:, h, :], gla_q[:, h, :]
                    for c in range(4):
                        at = 512 * (n % 3 % 2) + c * P
                        last = pe.matmul(pm[n % 3 // 2][:, at:at + P], lhs[:, c * P:(c + 1) * P], rhs[:, c * P:(c + 1) * P],
                                         start=True, stop=True)
                    last.then_inc(sem["gram_done"], 1)
                pe.wait_ge(sem["level_used"], LEVELS * (h + 1))
                pe.wait_ge(sem["q_done"], h + 1)
                pe.wait_ge(sem["s_done"], 10 * (h + 1))
                if h >= 1:
                    pe.wait_ge(sem["o_scaled"], 2 * h)
                for vt in range(2):
                    v0 = (2 * h + vt) * P
                    for c in range(4):
                        dst = pm[3][:, 512 * vt + c * P:512 * vt + (c + 1) * P]
                        cs = slice(c * P, (c + 1) * P)
                        pe.matmul(dst, gla_v[:, c, v0:v0 + P], pairs[:, h % 2, cs], start=True, stop=False)
                        pe.matmul(dst, state(0, c)[:, vt * P:(vt + 1) * P], q_in[:, 0, cs], start=False, stop=False)
                        last = pe.matmul(dst, state(1, c)[:, vt * P:(vt + 1) * P], q_in[:, 1, cs], start=False, stop=True)
                last.then_inc(sem["o_done"], 1)
                pe.wait_ge(sem["o_sq"], 2 * (h + 1))
                for vt in range(2):
                    last = pe.matmul(pm[1][:, 512:1024], ones[:, :], o_buf[:, vt, :], start=(vt == 0), stop=(vt == 1))
                last.then_inc(sem["o_ssq"], 1)

            pe.wait_ge(sem["o_ready"], KT)
            with pe.Fori(0, 2) as i:
                for u in range(4):
                    slab(S_GLA_OUT, i, u, o_hi2, o_lo2, LAT)
            pe.wait_ge(sem["summed"], 3 * KT)
            pe.wait_ge(sem["psum_free"], S_FFN1)
            stats(LAT)
            ffn(S_FFN1, 1, LAT)
            pe.wait_ge(sem["summed"], 4 * KT)
            pe.wait_ge(sem["psum_free"], N_SLABS)
            stats(LAT)

        @block.scalar
        def _(act):
            order = Order(act, sem["act_seq"])

            def split(s, slot):
                act.wait_ge(raw_in[slot % 4], 16 * (s // 4 + 1) if isinstance(s, int) else s)
                act.activation(w_hi[slot % 2][:, :], raw[slot % 4][:, :], ACT.Copy).then_inc(sem["split_hi"], 1)

            def step(base, i, u, evacuate):
                s = base + u + 4 * i
                act.wait_ge(sem["slab_done"], s + 1)
                nxt = base + u + 2
                if not (isinstance(s, int) and s + 2 >= N_SLABS):
                    act.wait_ge(raw_in[nxt % 4], 16 * (nxt // 4 + 1) + 16 * i)
                    act.activation(w_hi[nxt % 2][:, :], raw[nxt % 4][:, :], ACT.Copy).then_inc(sem["split_hi"], 1)
                evacuate(s, i, u, pm[(base + u) % 2])

            act.wait_ge(sem["vec_in"], 16)
            act.activation(cond[:, :, :].rearrange("p a b -> p (a b)"), col("cond", 0, 2 * KT), ACT.Silu).then_inc(
                sem["cond_done"], 1)
            for s in range(2):
                split(s, s)

            def modulate(n, first, tokens):
                act.wait_ge(sem["mod_f"], first + n + 1)
                act.activation(x_hi[:, n, 0:tokens], pool_t[:, n % 2, 0:tokens], ACT.Copy).then_inc(sem["x_hi_done"], 1)

            for n in range(KT):
                modulate(n, 0, TOK)

            def copy_qkv(s, i, u, src):
                act.activation(qkv[:, s, :], src[:, 0:TOK], ACT.Copy).then_inc(sem["psum_free"], 1)

            with act.Fori(0, 4) as i:
                for u in range(4):
                    step(0, i, u, copy_qkv)

            for h in range(6):
                act.wait_ge(sem["ssq_done"], h + 1)
                act.activation(norm[:, h, :], pm[h % 3][:, 0:TOK], ACT.Sqrt, bias=col("eps"), scale=1.0 / HEAD_DIM).then_inc(
                    sem["std_done"], 1)
            for t in range(TOK // P):
                act.wait_ge(sem["v_turned"], t + 1)
                act.activation(v_tok[:, t, :], pm[2][:, 0:4 * P], ACT.Copy).then_inc(sem["v_copied"], 1)

            def half_turn(n):
                width = len(UNITS[n]["tiles"]) * P
                act.wait_ge(sem["turned"], n + 1)
                act.activation(probs_t[:, n % 2, 0:width], pm[2][:, 0:width], ACT.Copy).then_inc(sem["turn_copied"], 1)

            def out_hi(o):
                act.wait_ge(sem["pv_done"], o + 1)
                k, a, b = OUTS[o]
                at = 512 * (o % 2)
                act.activation(x_hi[:, k, a:b], pm[3][:, at:at + b - a], ACT.Copy).then_inc(sem["o_hi"], 1)

            def exponentiate(n):
                u = UNITS[n]
                act.wait_ge(sem["shift_done"], n + 1)
                if n >= 2:
                    act.wait_ge(sem["turned"], n - 1)
                width = len(u["tiles"]) * P
                src = score[:, 0:width] if u["band"] is not None else pm[n % 2][:, 0:width]
                r = row[:, n % 8, :]
                act.activation(probs[:, n % 2, 0:width], src, ACT.Exp, bias=r[:, 1:2], scale=ATTN_SCALE,
                               accum_out=r[:, 2:3]).then_inc(sem["exp_done"], 1)
                if u["sink"] is not None:
                    act.activation(r[:, 3:4], col("sink", u["sink"]), ACT.Exp, bias=r[:, 1:2]).then_inc(
                        sem["exp_sink"], 1)

            for n in range(len(UNITS) + 1):
                if n < len(UNITS):
                    exponentiate(n)
                if n >= 1:
                    half_turn(n - 1)
                if n >= 2 and UNITS[n - 2]["last"]:
                    out_hi(UNITS[n - 2]["out"])
            out_hi(len(OUTS) - 1)

            first_res = [0]

            def residual_phase(base, layer, part, tokens):
                def evacuate(s, i, u, src):
                    n = i * 4 + u
                    done = first_res[0] + n - 1
                    if not (isinstance(done, int) and done < 1):
                        act.wait_ge(sem["residual"], done)
                    halves = HALVES if tokens == TOK else HALVES[:1]
                    for c, (a, b) in enumerate(halves):
                        last = act.activation(tmp[:, u % 2, a:b], src[:, a:b], ACT.Copy,
                                              scale=mods[:, layer, bass.ds(part + n, 1), c])
                    last.then_inc(sem["psum_free"], 1)
                if first_res[0] == 0 or base + KT == N_SLABS:
                    for j in range(8):
                        step(base + j, 0, 0, lambda s, i, u, src, j=j: evacuate(s, 0, j, src))
                else:
                    with act.Fori(0, 2) as i:
                        for u in range(4):
                            step(base, i, u, evacuate)
                first_res[0] += KT

            def norm_phase(c, tokens):
                act.wait_ge(sem["stat_done"], c + 1)
                act.activation(mean[:, 0:tokens], pm[0][:, 0:tokens], ACT.Copy).then_inc(sem["mean_out"], 1)
                act.wait_ge(sem["var_done"], c + 1)
                act.activation(rstd[:, 0:tokens], rstd[:, 0:tokens], ACT.Sqrt, bias=col("eps")).then_inc(sem["std2"], 1)
                for n in range(KT + 1):
                    if n < KT:
                        act.wait_ge(sem["centred"], KT * c + n + 1)
                        act.activation(h_res[:, n, 0:tokens], h_res[:, n, 0:tokens], ACT.Identity,
                                       bias=col("ln_b", c * KT + n), scale=col("ln_g", c * KT + n)).then_inc(
                            sem["h_ready"], 1)
                    if n >= 1 and c < 3:
                        modulate(n - 1, KT * (c + 1), TOK if c < 2 else LAT)

            residual_phase(S_ATTN_OUT, 0, G1, TOK)
            norm_phase(0, TOK)
            def ffn(base, layer, tokens):
                s0 = base
                done = FT * layer
                for g, tiles in enumerate(FF_GROUPS):
                    with act.Fori(0, tiles // 2) as i:
                        for u in range(4):
                            def evacuate(s, i, u, src):
                                j = sum(FF_GROUPS[:g]) + 2 * i + u // 2
                                tile = j + FT * (u % 2)
                                pair = done + 2 * i + u // 2
                                acc = (acc_g, acc_v)[u % 2]
                                act.wait_ge(sem["acc_free"], pair + 1)
                                act.activation(acc[:, 0:tokens], src[:, 0:tokens], ACT.Identity,
                                               bias=vec[:, bass.ds(VEC["conv_b"] + 2 * FT * layer + tile, 1)],
                                               scale=vec[:, bass.ds(VEC["conv_w"] + 2 * FT * (CONV_W * layer + 1) + tile, 1)]
                                               ).then_inc(sem["lin_done"], 1)
                                if u % 2 == 1:
                                    act.wait_ge(sem["psum_free"], s)
                                    act.activation(acc_g[:, 0:tokens], acc_g[:, 0:tokens], ACT.Silu).then_inc(
                                        sem["silu_done"], 1)
                                    act.wait_ge(sem["acc_free"], pair + 2)
                                    act.activation(hid_hi[:, bass.ds(2 * i + u // 2, 1), 0:tokens],
                                                   hid_f[:, 0:tokens].rearrange("p (a b) -> p a b", a=1), ACT.Copy).then_inc(sem["hid_split"], 1)
                            step(s0, i, u, evacuate)
                    done += tiles
                    s0 += 2 * tiles
                    residual_phase(s0, layer, G2, tokens)
                    s0 += KT

            ffn(S_FFN0, 0, TOK)
            norm_phase(1, TOK)

            def take_low(s, i, u, src):
                act.activation(low[0:2 * GLA_RANK, :], src[0:2 * GLA_RANK, 0:TOK], ACT.Copy).then_inc(sem["psum_free"], 1)
                act.wait_ge(sem["psum_free"], s + 1)
                act.sem_inc(sem["low_done"], 1)

            def take_key(s, i, u, src):
                act.activation(gla_k[:, u - 1, :], src[:, 0:TOK], ACT.Copy).then_inc(sem["psum_free"], 1)

            def softplus(j):
                act.wait_ge(sem["logit_done"], j + 1)
                if j >= 2:
                    act.wait_ge(sem["ld_done"], j - 1)
                t = soft[:, j % 2, :]
                act.activation(t, pm[2 + j % 2][:, 0:TOK], ACT.Abs, bias=col("b_a", j)).then_inc(sem["abs_done"], 1)
                act.wait_ge(sem["abs_done"], j + 1)
                order.mark(act.activation(t, t, ACT.Exp, scale=-1.0))
                order.wait()
                act.activation(t, t, ACT.Ln, bias=1.0).then_inc(sem["log_done"], 1)

            step(S_GLA, 0, 0, take_low)
            for n in range(GLA_HEADS):
                step(S_GLA, 0, n + 1, take_key)
                softplus(2 * n)
                softplus(2 * n + 1)
            act.wait_ge(sem["ld_done"], 2 * GLA_HEADS)
            with act.Fori(0, 2) as i:
                def take_value(s, i, u, src):
                    act.wait_ge(sem["v_turned"], TOK // P + u - 1 + 4 * i)
                    act.activation(v_turn[:, u % 2, :], src[:, 0:TOK], ACT.Copy).then_inc(sem["psum_free"], 1)

                def copy_value(u):
                    act.wait_ge(sem["v_turned"], TOK // P + u + 1 + 4 * i)
                    act.activation(gla_v[:, :, bass.ds(4 * P * i + u * P, P)],
                                   pm[2 + u % 2][:, 0:TOK].rearrange("p (a b) -> p a b", b=P), ACT.Copy).then_inc(
                        sem["v_copied"], 1)

                for u in range(4):
                    step(S_GLA + 1 + GLA_HEADS, i, u, take_value)
                    if u >= 1:
                        copy_value(u - 1)
                copy_value(3)

            def take_query(s, i, u, src):
                act.activation(gla_q[:, u, :], src[:, 0:LAT], ACT.Copy, scale=P ** -0.5).then_inc(sem["psum_free"], 1)

            def take_gate(s, i, u, src):
                act.activation(gla_g[:, bass.ds(4 * i + u, 1), :], src[:, 0:LAT].rearrange("p (a b) -> p a b", a=1),
                               ACT.Silu).then_inc(sem["psum_free"], 1)

            for u in range(4):
                step(S_GLA + N_GLA_ALL, 0, u, take_query)
            with act.Fori(0, 2) as i:
                for u in range(4):
                    step(S_GLA + N_GLA_ALL + 4, i, u, take_gate)

            INV = 1.0 / 16.0
            act.activation(decay[:, :, :, :].rearrange("p a b c -> p (a b c)"),
                           chunk_sum[:, :, :, :].rearrange("p a b c -> p (a b c)"), ACT.Exp, scale=INV).then_inc(
                sem["decay_done"], 1)
            act.wait_ge(sem["slab_done"], S_GLA_OUT)

            def finish_head(h):
                for vt in range(2):
                    act.wait_ge(sem["o_gated"], 2 * h + vt + 1)
                    act.activation(o_hi2[:, 2 * h + vt, :], o_buf[:, vt, :], ACT.Copy).then_inc(sem["o_hi_done"], 1)

            for h in range(GLA_HEADS):
                for z in range(2):
                    q = 2 * h + z
                    if z == 0:
                        act.wait_ge(sem["k_diff"], h + 1)
                        src = k_out[:, :]
                    else:
                        act.wait_ge(sem["k_turned"], q)
                        src = cum[:, 1, h, :]
                    act.activation(k_out[:, :], src, ACT.Exp, scale=INV).then_inc(sem["k_exp"], 1)
                    act.wait_ge(sem["k_turned"], q + 1)
                    if q >= 1:
                        act.wait_ge(sem["s_prod"], q)
                    if z == 0 and h >= 1:
                        act.wait_ge(sem["o_ready"], 2 * h)
                    act.activation(k_tok[:, :, :], pm[2][:, 0:5 * P].rearrange("p (a b) -> p a b", b=P), ACT.Copy).then_inc(
                        sem["k_copied"], 1)
                act.wait_ge(sem["q_diff"], h + 1)
                act.activation(q_in[:, 0, :], cum[:, 0, h, 0:LAT], ACT.Exp, scale=INV)
                act.activation(q_in[:, 1, :], q_in[:, 1, :], ACT.Exp, scale=INV).then_inc(sem["q_exp"], 1)
                act.wait_ge(sem["gram_done"], LEVELS * h + 1)
                at = LEVELS * h % 3
                act.activation(pairs[:, h % 2, :], pm[at // 2][:, 512 * (at % 2):512 * (at % 2) + LAT], ACT.Copy,
                               scale=2.0).then_inc(sem["level_used"], 1)
                for lv in range(LEVELS - 1):
                    m = (LEVELS - 1) * h + lv
                    act.wait_ge(sem["diff_done"], m + 1)
                    act.activation(fade[:, m % 3, :], fade[:, m % 3, :], ACT.Exp, scale=INV).then_inc(sem["fade_done"], 1)
                act.wait_ge(sem["o_done"], h + 1)
                for vt in range(2):
                    act.activation(o_buf[:, vt, :], pm[3][:, 512 * vt:512 * (vt + 1)], ACT.Square).then_inc(sem["o_sq"], 1)
                act.wait_ge(sem["o_ssq"], h + 1)
                act.activation(o_rms[:, :], pm[1][:, 512:1024], ACT.Sqrt, bias=col("eps"), scale=1.0 / (2 * P)).then_inc(
                    sem["o_std"], 1)
                finish_head(h)

            residual_phase(S_GLA_OUT, 1, G1, LAT)
            norm_phase(2, LAT)
            ffn(S_FFN1, 1, LAT)
            norm_phase(3, LAT)

        @block.vector
        def _(dve):
            order = Order(dve, sem["dve_seq"])

            def rest(s, nxt, i=0):
                dve.wait_ge(sem["split_hi"], s + 1)
                dve.tensor_tensor(w_lo[nxt % 2][:, :], raw[nxt % 4][:, :], w_hi[nxt % 2][:, :].bitcast(FP32),
                                  ALU.subtract).then_inc(sem["split_lo"], 1)

            def step(base, i, u, evacuate=None):
                s = base + u + 4 * i
                if not (isinstance(s, int) and s + 2 >= N_SLABS):
                    rest(s + 2, base + u + 2)
                if evacuate is not None:
                    evacuate(s, i, u, pm[(base + u) % 2])

            dve.memset(mean_w[:, :], 1.0 / D_MODEL).then_inc(sem["ones_done"], 1)
            dve.memset(ones[:, :], 1.0).then_inc(sem["ones_done"], 1)
            dve.memset(acc_g[:, 0:1], 0.0).then_inc(sem["acc_free"], 1)

            def take_mods(layer, first, count, scales):
                got = mods[:, layer, first:first + count, :]
                at = 512 + 2 * (first + ADA_TILES * layer)
                bias = col("ada_b", ADA_TILES * layer + first, count)
                dve.wait_ge(sem["ada_done"], ADA_TILES * layer + first + count)
                for c in range(2):
                    last = dve.tensor_tensor(got[:, :, c], pm[3][:, at:at + 2 * count].rearrange("p (a b) -> p a b", b=2)[:, :, c], bias, ALU.add)
                order.mark(last)
                order.wait()
                dve.tensor_scalar(mods[:, layer, scales:scales + KT, :], mods[:, layer, scales:scales + KT, :], 1.0,
                                  None, ALU.add).then_inc(sem["mods_done"], 1)

            dve.wait_ge(sem["vec_in"], 16)
            take_mods(0, 0, 16, SC1)
            for s in range(2):
                rest(s, s)

            def x_rest(n, first, tokens):
                dve.wait_ge(sem["x_hi_done"], first + n + 1)
                dve.tensor_tensor(x_lo[:, n, 0:tokens], pool_t[:, n % 2, 0:tokens], x_hi[:, n, 0:tokens].bitcast(FP32),
                                  ALU.subtract).then_inc(sem["x_ready"], 1)

            for n in range(KT):
                x_rest(n, 0, TOK)

            with dve.Fori(0, 4) as i:
                for u in range(4):
                    step(0, i, u)

            def rotate(h, count):
                z = qkv[:, h, 0:LAT]
                b = count % 2
                if count >= 2:
                    dve.wait_ge(sem["roped"], count - 1)
                dve.tensor_tensor(rope_s[0:64, b, :], z[64:128, :], rope[64:128, 1, :], ALU.mult)
                order.mark(dve.tensor_tensor(rope_s[64:128, b, :], z[0:64, :], rope[0:64, 1, :], ALU.mult))
                dve.tensor_tensor(rope_c[:, b, :], z, rope[:, 0, :], ALU.mult).then_inc(sem["rope_p"], 1)
                order.wait()
                dve.wait_ge(sem["rope_p"], count + 1)
                dve.tensor_tensor(z, rope_c[:, b, :], rope_s[:, b, :], ALU.add).then_inc(sem["roped"], 1)

            dve.wait_ge(sem["const_in"], 48)
            dve.wait_ge(sem["psum_free"], N_ATTN_IN)
            count = 0
            for h in range(HEAD_OF["bq"], HEAD_OF["bk"] + N_KV):
                rotate(h, count)
                count += 1
            for h in range(6):
                dve.wait_ge(sem["std_done"], h + 1)
                order.mark(dve.reciprocal(norm[:, h, :], norm[:, h, :]))
                order.wait()
                g = col("q_norm") if h < N_HEADS else col("k_norm")
                dve.scalar_tensor_tensor(qkv[:, h, :], qkv[:, h, :], g, norm[:, h, :], ALU.mult, ALU.mult).then_inc(
                    sem["normed"], 1)
                dve.wait_ge(sem["normed"], h + 1)
                rotate(h, count)
                count += 1
            take_mods(0, 16, 32, SC2)

            def out_lo(o):
                k, a, b = OUTS[o]
                at = 512 * (o % 2)
                dve.wait_ge(sem["o_hi"], o + 1)
                ins = dve.tensor_tensor(x_lo[:, k, a:b], pm[3][:, at:at + b - a], x_hi[:, k, a:b].bitcast(FP32), ALU.subtract)
                ins.then_inc(sem["pv_copied"], 1)

            def shift(n):
                u = UNITS[n]
                width = len(u["tiles"]) * P
                r = row[:, n % 8, :]
                dve.wait_ge(sem["score_done"], n + 1)
                src = pm[n % 2]
                if u["band"] is not None:
                    at, w = u["band"]
                    if n >= 1:
                        dve.wait_ge(sem["exp_done"], n)
                    dve.tensor_tensor(score[:, 0:w], src[:, 0:w], band[:, at:at + w], ALU.add)
                    order.mark(dve.tensor_copy(score[:, w:width], src[:, w:width]))
                    order.wait()
                    src = score
                order.mark(dve.tensor_reduce(r[:, 0:1], src[:, 0:width], AX.X, ALU.max))
                order.wait()
                if u["sink"] is None:
                    dve.tensor_scalar(r[:, 1:2], r[:, 0:1], -ATTN_SCALE, None, ALU.mult).then_inc(sem["shift_done"], 1)
                else:
                    order.mark(dve.tensor_scalar(r[:, 4:5], r[:, 0:1], ATTN_SCALE, col("sink", u["sink"]), ALU.mult, ALU.max))
                    order.wait()
                    dve.tensor_scalar(r[:, 1:2], r[:, 4:5], -1.0, None, ALU.mult).then_inc(sem["shift_done"], 1)

            def normalise(n):
                u = UNITS[n]
                width = len(u["tiles"]) * P
                r = row[:, n % 8, :]
                dve.wait_ge(sem["exp_done"], n + 1)
                total = r[:, 2:3]
                if u["sink"] is not None:
                    dve.wait_ge(sem["exp_sink"], sum(x["sink"] is not None for x in UNITS[:n + 1]))
                    order.mark(dve.tensor_tensor(r[:, 5:6], r[:, 2:3], r[:, 3:4], ALU.add))
                    order.wait()
                    total = r[:, 5:6]
                order.mark(dve.reciprocal(r[:, 6:7], total))
                order.wait()
                dve.tensor_scalar(probs[:, n % 2, 0:width], probs[:, n % 2, 0:width], r[:, 6:7], None,
                                  ALU.mult).then_inc(sem["probs_done"], 1)

            for n in range(len(UNITS) + 1):
                if n < len(UNITS):
                    shift(n)
                if n >= 1:
                    normalise(n - 1)
                if n >= 3 and UNITS[n - 3]["last"]:
                    out_lo(UNITS[n - 3]["out"])
            out_lo(len(OUTS) - 2) if UNITS[len(UNITS) - 2]["last"] else None
            out_lo(len(OUTS) - 1)

            def residual_phase(base, tokens, scale):
                def evacuate(s, i, u, src):
                    n = 4 * i + u
                    dve.wait_ge(sem["psum_free"], s + 1)
                    dve.scalar_tensor_tensor(h_res[:, bass.ds(n, 1), 0:tokens].rearrange("p a b -> p (a b)"),
                                             h_res[:, bass.ds(n, 1), 0:tokens].rearrange("p a b -> p (a b)"), scale,
                                             tmp[:, u % 2, 0:tokens], ALU.mult, ALU.add).then_inc(sem["residual"], 1)
                if base + KT == N_SLABS:
                    for j in range(8):
                        step(base + j, 0, 0, lambda s, i, u, src, j=j: evacuate(s, 0, j, src))
                else:
                    with dve.Fori(0, 2) as i:
                        for u in range(4):
                            step(base, i, u, evacuate)

            def norm_phase(c, tokens):
                dve.wait_ge(sem["mean_out"], c + 1)
                order.mark(dve.tensor_tensor(rstd[:, 0:tokens], mean[:, 0:tokens], mean[:, 0:tokens], ALU.mult))
                order.wait()
                dve.tensor_tensor(rstd[:, 0:tokens], pm[1][:, 0:tokens], rstd[:, 0:tokens], ALU.subtract).then_inc(
                    sem["var_done"], 1)
                dve.wait_ge(sem["std2"], c + 1)
                order.mark(dve.reciprocal(rstd[:, 0:tokens], rstd[:, 0:tokens]))
                order.wait()
                for n in range(KT + 1):
                    if n < KT:
                        order.mark(dve.tensor_tensor(h_res[:, n, 0:tokens], h_res[:, n, 0:tokens], mean[:, 0:tokens], ALU.subtract))
                        order.wait()
                        dve.tensor_tensor(h_res[:, n, 0:tokens], h_res[:, n, 0:tokens], rstd[:, 0:tokens], ALU.mult).then_inc(
                            sem["centred"], 1)
                    if n >= 1 and c < 3:
                        x_rest(n - 1, KT * (c + 1), TOK if c < 2 else LAT)

            residual_phase(S_ATTN_OUT, TOK, ALPHA)
            norm_phase(0, TOK)
            take_mods(1, 0, 24, SC1)

            def ffn(base, layer, tokens):
                s0 = base
                done = FT * layer
                for g, tiles in enumerate(FF_GROUPS):
                    with dve.Fori(0, tiles // 2) as i:
                        order.enter(i, 4)
                        for u in range(4):
                            def evacuate(s, i, u, src):
                                j = sum(FF_GROUPS[:g]) + 2 * i + u // 2
                                tile = j + FT * (u % 2)
                                pair = done + 2 * i + u // 2
                                acc = (acc_g, acc_v)[u % 2]
                                before = vec[:, bass.ds(VEC["conv_w"] + 2 * FT * (CONV_W * layer) + tile, 1)]
                                after = vec[:, bass.ds(VEC["conv_w"] + 2 * FT * (CONV_W * layer + 2) + tile, 1)]
                                dve.wait_ge(sem["lin_done"], 2 * pair + u % 2 + 1)
                                halves = HALVES if tokens == TOK else HALVES[:1]
                                for a, b in halves:
                                    last = dve.scalar_tensor_tensor(acc[:, a + 1:b], src[:, a:b - 1], before, acc[:, a + 1:b],
                                                                    ALU.mult, ALU.add)
                                order.mark(last)
                                order.wait()
                                for a, b in halves:
                                    last = dve.scalar_tensor_tensor(acc[:, a:b - 1], src[:, a + 1:b], after, acc[:, a:b - 1],
                                                                    ALU.mult, ALU.add)
                                last.then_inc(sem["psum_free"], 1)
                                if u % 2 == 1:
                                    dve.wait_ge(sem["psum_free"], s + 1)
                                    dve.wait_ge(sem["silu_done"], pair + 1)
                                    dve.tensor_tensor(hid_f[:, 0:tokens], acc_g[:, 0:tokens], acc_v[:, 0:tokens],
                                                      ALU.mult).then_inc(sem["acc_free"], 1)
                                    dve.wait_ge(sem["hid_split"], pair + 1)
                                    dve.tensor_tensor(hid_lo[:, bass.ds(2 * i + u // 2, 1), 0:tokens].rearrange("p a b -> p (a b)"),
                                                      hid_f[:, 0:tokens],
                                                      hid_hi[:, bass.ds(2 * i + u // 2, 1), 0:tokens].rearrange("p a b -> p (a b)").bitcast(FP32),
                                                      ALU.subtract).then_inc(sem["hid_ready"], 1)
                            step(s0, i, u, evacuate)
                        order.leave(tiles // 2)
                    done += tiles
                    s0 += 2 * tiles
                    residual_phase(s0, tokens, ALPHA if g == 0 else 1.0)
                    s0 += KT

            ffn(S_FFN0, 0, TOK)
            norm_phase(1, TOK)
            take_mods(1, 24, 24, SC2)

            order.mark(dve.memset(restart[:, :], 1.0))
            order.wait()
            order.mark(dve.memset(chunks(restart[:, :])[:, :, 0:1], 0.0))

            def decays(j):
                z, h = j // GLA_HEADS, j % GLA_HEADS
                dve.wait_ge(sem["abs_done"], j + 1)
                if j >= 1:
                    dve.wait_ge(sem["ld_done"], j)
                order.mark(dve.tensor_scalar(clipped[:, :], pm[2 + j % 2][:, 0:TOK], col("b_a", j), 0.0, ALU.add, ALU.min))
                order.wait()
                dve.wait_ge(sem["log_done"], j + 1)
                order.mark(dve.tensor_tensor(clipped[:, :], clipped[:, :], soft[:, j % 2, :], ALU.subtract))
                order.wait()
                order.mark(dve.tensor_tensor_scan(cum[:, z, h, :], restart[:, :], clipped[:, :], 0.0, ALU.mult, ALU.add))
                order.wait()
                last = dve.tensor_copy(chunk_sum[:, z, h, :].unsqueeze(2), chunks(cum[:, z, h, :])[:, :, P - 1:P])
                if z == 1:
                    order.mark(last)
                    order.wait()
                    last = dve.tensor_tensor(cum[:, z, h, :], cum[:, z, h, :], clipped[:, :], ALU.subtract)
                last.then_inc(sem["ld_done"], 1)

            step(S_GLA, 0, 0)
            for n in range(GLA_HEADS):
                step(S_GLA, 0, n + 1)
                decays(2 * n)
                decays(2 * n + 1)
            with dve.Fori(0, 2) as i:
                for u in range(4):
                    step(S_GLA + 1 + GLA_HEADS, i, u)
            with dve.Fori(0, 3) as i:
                for u in range(4):
                    step(S_GLA + N_GLA_ALL, i, u)

            dve.wait_ge(sem["psum_free"], S_GLA_OUT)
            dve.wait_ge(sem["v_copied"], TOK // P + 8)
            dve.wait_ge(sem["decay_done"], 1)
            dve.wait_ge(sem["level_in"], 16)
            dve.tensor_copy(level[:, :, :], level_f[:, :, :]).then_inc(sem["level_done"], 1)
            dve.wait_ge(sem["level_done"], 1)

            def totals(z, h, n):
                return chunk_sum[:, z, h, 0:n].unsqueeze(2).to_broadcast([P, n, P])

            def level_diff(h, lv):
                b, z = lv // 2, lv % 2
                m = (LEVELS - 1) * h + lv
                if m >= 3:
                    dve.wait_ge(sem["both_done"], m - 2)
                left, right, mid = segments(b, z, h)
                to_left, to_right, _ = segments(b, z, h, fade[:, m % 3, :])
                dve.tensor_tensor(to_left, mid, left, ALU.subtract)
                dve.tensor_tensor(to_right, right, mid, ALU.subtract).then_inc(sem["diff_done"], 1)

            for h in range(GLA_HEADS):
                if h >= 1:
                    dve.wait_ge(sem["k_turned"], 2 * h)
                dve.tensor_tensor(chunks(k_out[:, :]), totals(0, h, 6), chunks(cum[:, 0, h, :]), ALU.subtract).then_inc(
                    sem["k_diff"], 1)
                for z in range(2):
                    for j in range(5):
                        n = 5 * (2 * h + z) + j
                        c = SCAN[z][j]
                        dst = state(z, STATE[z][j])
                        dve.wait_ge(sem["s_prod"], 2 * h + z + 1)
                        if n == 10 * h and h >= 1:
                            dve.wait_ge(sem["o_done"], h)
                        src = state_sum(j)
                        if j == 0:
                            dve.tensor_copy(dst, src).then_inc(sem["s_done"], 1)
                        else:
                            dve.wait_ge(sem["s_done"], n)
                            dve.scalar_tensor_tensor(dst, state(z, STATE[z][j - 1]), decay[:, z, h, c:c + 1], src,
                                                     ALU.mult, ALU.add).then_inc(sem["s_done"], 1)
                dve.tensor_tensor(chunks(q_in[:, 1, :]), totals(1, h, 4), chunks(cum[:, 1, h, 0:LAT]), ALU.subtract).then_inc(
                    sem["q_diff"], 1)
                level_diff(h, 0)
                level_diff(h, 1)
                for lv in range(LEVELS - 1):
                    if lv + 2 < LEVELS - 1:
                        level_diff(h, lv + 2)
                    n = LEVELS * h + lv + 1
                    dve.wait_ge(sem["gram_done"], n + 1)
                    dve.wait_ge(sem["level_used"], n)
                    at = n % 3
                    dve.copy_predicated(chunks(pairs[:, h % 2, :]), level[:, lv, :].unsqueeze(1).to_broadcast([P, 4, P]),
                                        chunks(pm[at // 2][:, 512 * (at % 2):512 * (at % 2) + LAT])).then_inc(
                        sem["level_used"], 1)
                dve.wait_ge(sem["o_std"], h + 1)
                dve.reciprocal(o_rms[:, :], o_rms[:, :]).then_inc(sem["o_rms"], 1)
                dve.wait_ge(sem["o_rms"], h + 1)
                for vt in range(2):
                    dve.scalar_tensor_tensor(o_buf[:, vt, :], pm[3][:, 512 * vt:512 * (vt + 1)], col("head_norm", vt),
                                             o_rms[:, :], ALU.mult, ALU.mult).then_inc(sem["o_scaled"], 1)
                for vt in range(2):
                    dve.wait_ge(sem["o_hi_done"], 2 * h + vt + 1)
                    dve.tensor_tensor(o_lo2[:, 2 * h + vt, :], o_buf[:, vt, :], o_hi2[:, 2 * h + vt, :].bitcast(FP32),
                                      ALU.subtract).then_inc(sem["o_ready"], 1)

            residual_phase(S_GLA_OUT, LAT, ALPHA)
            norm_phase(2, LAT)
            ffn(S_FFN1, 1, LAT)
            norm_phase(3, LAT)

        @block.gpsimd
        def _(pool):
            order = Order(pool, sem["pool_seq"])

            def modulated(n, first, layer, scale, shift_, tokens):
                if first + n >= 2:
                    pool.wait_ge(sem["x_ready"], first + n - 1)
                for c, (a, b) in enumerate(HALVES if tokens == TOK else HALVES[:1]):
                    last = pool.tensor_scalar(pool_t[:, n % 2, a:b], h_res[:, n, a:b], mods[:, layer, scale + n, c:c + 1],
                                              mods[:, layer, shift_ + n, c:c + 1], ALU.mult, ALU.add)
                last.then_inc(sem["mod_f"], 1)

            pool.wait_ge(sem["x_loaded"], 16)
            pool.wait_ge(sem["mods_done"], 1)
            for n in range(KT):
                modulated(n, 0, 0, SC1, SH1, TOK)

            for h in range(6):
                pool.wait_ge(sem["psum_free"], h + 1)
                if h == 0:
                    pool.wait_ge(sem["ada_done"], 16)
                dst = square[:, h, :] if h < 5 else square_5[:, :]
                pool.tensor_tensor(dst, qkv[:, h, :], qkv[:, h, :], ALU.mult).then_inc(sem["squared"], 1)

            def sums_phase(first_res, c, tokens):
                order.mark(pool.memset(sum1[:, :], 0.0))
                order.mark(pool.memset(sum2[:, :], 0.0))
                order.wait()
                with pool.Fori(0, 2) as i:
                    order.enter(i, 8)
                    for u in range(4):
                        n = 4 * i + u
                        pool.wait_ge(sem["residual"], first_res + n + 1)
                        src = h_res[:, bass.ds(n, 1), 0:tokens].rearrange("p a b -> p (a b)")
                        order.mark(pool.tensor_tensor(pool_t[:, 0, 0:tokens], src, src, ALU.mult))
                        order.mark(pool.tensor_tensor(sum1[:, 0:tokens], sum1[:, 0:tokens], src, ALU.add))
                        order.wait()
                        pool.tensor_tensor(sum2[:, 0:tokens], sum2[:, 0:tokens], pool_t[:, 0, 0:tokens],
                                           ALU.add).then_inc(sem["summed"], 1)
                        pool.wait_ge(sem["summed"], KT * c + n + 1)
                    order.leave(2)

            pool.wait_ge(sem["pv_copied"], len(OUTS))
            sums_phase(0, 0, TOK)
            for n in range(KT):
                pool.wait_ge(sem["h_ready"], n + 1)
                modulated(n, KT, 0, SC2, SH2, TOK)
            pool.wait_ge(sem["x_ready"], 2 * KT)
            sums_phase(KT * 3, 1, TOK)
            pool.wait_ge(sem["mods_done"], 3)
            for n in range(KT):
                pool.wait_ge(sem["h_ready"], KT + n + 1)
                modulated(n, 2 * KT, 1, SC1, SH1, TOK)

            pool.wait_ge(sem["psum_free"], S_GLA_OUT)
            for h in range(GLA_HEADS):
                for z in range(2):
                    pool.wait_ge(sem["k_exp"], 2 * h + z + 1)
                    pool.tensor_tensor(k_out[:, :], k_out[:, :], gla_k[:, h, :], ALU.mult).then_inc(sem["k_done"], 1)
                pool.wait_ge(sem["q_exp"], h + 1)
                for z in range(2):
                    last = pool.tensor_tensor(q_in[:, z, :], q_in[:, z, :], gla_q[:, h, :], ALU.mult)
                last.then_inc(sem["q_done"], 1)
                for lv in range(LEVELS - 1):
                    b, z = lv // 2, lv % 2
                    m = (LEVELS - 1) * h + lv
                    pool.wait_ge(sem["fade_done"], m + 1)
                    if m >= 2:
                        pool.wait_ge(sem["gram_done"], LEVELS * ((m - 2) // (LEVELS - 1)) + (m - 2) % (LEVELS - 1) + 2)
                    sides = (gla_k, gla_q) if z == 0 else (gla_q, gla_k)
                    for side in range(2):
                        last = pool.tensor_tensor(segments(b, z, h, both[:, m % 2, :])[side],
                                                  segments(b, z, h, fade[:, m % 3, :])[side],
                                                  segments(b, z, h, sides[side][:, h, 0:LAT])[side], ALU.mult)
                    last.then_inc(sem["both_done"], 1)
                for vt in range(2):
                    pool.wait_ge(sem["o_scaled"], 2 * h + vt + 1)
                    pool.tensor_tensor(o_buf[:, vt, :], o_buf[:, vt, :], gla_g[:, 2 * h + vt, :], ALU.mult).then_inc(
                        sem["o_gated"], 1)

            pool.wait_ge(sem["o_ready"], KT)
            sums_phase(KT * 4, 2, LAT)
            pool.wait_ge(sem["mods_done"], 4)
            for n in range(KT):
                pool.wait_ge(sem["h_ready"], 2 * KT + n + 1)
                modulated(n, 3 * KT, 1, SC2, SH2, LAT)
            pool.wait_ge(sem["x_ready"], 4 * KT)
            sums_phase(KT * 7, 3, LAT)


UNITS, OUTS = [], []


def _units():
    heads = [("b", h) for h in range(N_HEADS)] + [("a", h) for h in range(N_HEADS)]
    for group, h in heads:
        kv = h // (N_HEADS // N_KV)
        for first, last, tokens in ((0, LAT, "lat"), (LAT, TOK, "ctx")):
            blocks = list(range(first, last, P))
            for q0 in blocks:
                band = None
                if tokens == "ctx":
                    keys = [(LAT, TOK)]
                elif group == "a":
                    keys = [(0, LAT), (LAT, TOK)]
                else:
                    lo, hi = max(q0 - P, 0), min(q0 + 2 * P, LAT)
                    keys = [(lo, hi), (LAT, TOK)]
                    band = (lo - (q0 - P), hi - lo)
                spans, at = [], 0
                for a, b in keys:
                    while a < b:
                        n = min(b - a, 512 - at % 512)
                        spans.append((at, a, a + n))
                        at, a = at + n, a + n
                tiles = [t for a, b in keys for t in range(a // P, b // P)]
                UNITS.append(dict(q=HEAD_OF[group + "q"] + h, k=HEAD_OF[group + "k"] + kv,
                                  v=kv + (N_KV if group == "b" else 0), q0=q0, spans=spans, tiles=tiles, band=band,
                                  sink=h if group == "b" else None, out=len(OUTS), o0=q0 - first,
                                  first=q0 == first, last=q0 == blocks[-1]))
            OUTS.append((h + (N_HEADS if group == "b" else 0), first, last))


_units()


def _slabs(attn_w_in, attn_w_out, gla_w_in, gla_w_a1, gla_w_out, ffn_w_up, ffn_w_down):
    import numpy as np

    def cut(w, n, rows=None):
        w = w[:, n * P:(n + 1) * P] if rows is None else w[rows[0] * P:rows[1] * P, n * P:(n + 1) * P]
        full = np.zeros((KT * P, P), w.dtype)
        full[:w.shape[0], :w.shape[1]] = w
        return full.reshape(KT, P, P).transpose(1, 0, 2).reshape(P, KT * P)

    def ffn(layer):
        got, first = [], 0
        for tiles in FF_GROUPS:
            for j in range(first, first + tiles):
                got += [cut(ffn_w_up[layer], j), cut(ffn_w_up[layer], FT + j)]
            got += [cut(ffn_w_down[layer], n, (first, first + tiles)) for n in range(KT)]
            first += tiles
        return got

    got = [cut(attn_w_in[0], n) for n in ATTN_COLS] + [cut(attn_w_out[0], n) for n in range(KT)] + ffn(0)
    rank = np.concatenate([gla_w_a1[0, 0], gla_w_a1[0, 1]], axis=1)
    got += [cut(rank, 0)] + [cut(gla_w_in[0], n) for n in (*range(4, 16), *range(0, 4), *range(16, 24))]
    got += [cut(gla_w_out[0], n) for n in range(KT)] + ffn(1)
    return np.stack(got)


def _columns(a):
    return a.reshape(-1, P).T


def kernel(x, c, ctx, c_ctx, ada_w, ada_b, ln_g, ln_b, ffn_w_up, ffn_conv_w, ffn_conv_b, ffn_w_down,
           attn_w_in, attn_q_norm, attn_k_norm, attn_sink, attn_w_out,
           gla_w_in, gla_w_a1, gla_w_a2, gla_b_a, gla_head_norm, gla_w_out):
    import numpy as np
    import concourse.bacc as bacc
    from concourse.bass_utils import run_bass_kernel_spmd

    arrays = _arrays(np, x, c, ctx, c_ctx, ada_w, ada_b, ln_g, ln_b, ffn_w_up, ffn_conv_w, ffn_conv_b, ffn_w_down,
                     attn_w_in, attn_q_norm, attn_k_norm, attn_sink, attn_w_out,
                     gla_w_in, gla_w_a1, gla_w_a2, gla_b_a, gla_head_norm, gla_w_out)
    nc = bacc.Bacc("TRN2", target_bir_lowering=False, num_devices=1)
    build(nc, arrays)
    got = run_bass_kernel_spmd(nc, [arrays], core_ids=[0]).results[0]["out"]
    return np.ascontiguousarray(np.asarray(got).transpose(2, 1, 0).reshape(1, LAT, D_MODEL))


def build(nc, arrays):
    args = [nc.dram_tensor(n, a.shape, mybir.dt.from_np(a.dtype), kind="ExternalInput").ap() for n, a in arrays.items()]
    args.append(nc.dram_tensor("out", [P, KT, LAT], FP32, kind="ExternalOutput").ap())
    trunk(nc, *args)


def _arrays(np, x, c, ctx, c_ctx, ada_w, ada_b, ln_g, ln_b, ffn_w_up, ffn_conv_w, ffn_conv_b, ffn_w_down,
            attn_w_in, attn_q_norm, attn_k_norm, attn_sink, attn_w_out,
            gla_w_in, gla_w_a1, gla_w_a2, gla_b_a, gla_head_norm, gla_w_out):
    tokens = np.concatenate([x[0], ctx[0]], axis=0)
    cond = np.stack([_columns(c[0]), _columns(c_ctx)], axis=-1).reshape(P, 2 * KT)
    vec = np.concatenate([
        cond, _columns(ada_b), _columns(ln_g), _columns(ln_b), _columns(ffn_conv_w), _columns(ffn_conv_b),
        _columns(attn_q_norm), _columns(attn_k_norm), np.broadcast_to(attn_sink, (P, N_HEADS)),
        _columns(gla_b_a), _columns(gla_head_norm), np.full((P, 1), EPS, np.float32)], axis=1)
    ada = ada_w.reshape(2, KT, P, ADA_TILES // 2, 2, P).transpose(0, 3, 2, 4, 1, 5).reshape(ADA_TILES, P, 2 * KT * P)
    a2 = np.zeros((2 * GLA_RANK, 2, GLA_HEADS * P), np.float32)
    for z in range(2):
        a2[z * GLA_RANK:(z + 1) * GLA_RANK, z] = gla_w_a2[0, z]

    t = np.arange(LAT)
    freq = np.power(np.float32(ROPE_THETA), -np.arange(HEAD_DIM // 4, dtype=np.float32) * 2.0 / (HEAD_DIM // 2))
    freq = freq.astype(np.float32)
    angle = np.concatenate([(t // GRID_W).astype(np.float32)[:, None] * freq,
                            (t % GRID_W).astype(np.float32)[:, None] * freq], axis=-1).T
    rope = np.stack([np.concatenate([np.cos(angle)] * 2), np.concatenate([np.sin(angle), -np.sin(angle)])], axis=1)
    q, k = np.arange(P)[:, None], np.arange(3 * P)[None, :] - P
    band = np.where(np.abs(k - q) <= WINDOW, 0.0, MASKED)
    first, second = np.arange(P)[:, None], np.arange(P)[None, :]
    level = []
    for b in range(GLA_LEVELS):
        m = 1 << b
        pair = (first // (2 * m) == second // (2 * m)) & (first // m != second // m)
        level += [pair & (first < second), pair & (first > second)]
    out = {
        "x": tokens.T.reshape(KT, P, TOK).transpose(1, 0, 2), "vec": vec,
        "slabs": _slabs(attn_w_in, attn_w_out, gla_w_in, gla_w_a1, gla_w_out, ffn_w_up, ffn_w_down),
        "ada": ada, "rope": rope, "band": band, "eye": np.eye(P), "a2": a2,
        "level": np.stack(level, axis=1)}
    return {n: np.ascontiguousarray(a, dtype=np.float32) for n, a in out.items()}
```

```python
from contextlib import ExitStack

import concourse.bass as bass
from concourse import mybir

FP32 = mybir.dt.float32
FP32R = mybir.dt.float32r
ALU = mybir.AluOpType
ACT = mybir.ActivationFunctionType
AX = mybir.AxisListType

P = 128
D_MODEL = 1024
KT = D_MODEL // P
LAT = 512
CTX = 256
TOK = LAT + CTX
GRID_W = 64
HEAD_DIM = 128
WINDOW = 128
N_HEADS = 4
N_KV = 2
D_FF = 2816
FT = D_FF // P
FF_GROUPS = (8, 8, 6)
CONV_W = 3
GLA_HEADS = 4
GLA_RANK = 16
GLA_CHUNK = 128
GLA_LEVELS = 7
ATTN_SCALE = HEAD_DIM ** -0.5
ALPHA = 4 ** 0.25
EPS = 1e-6
ROPE_THETA = 10000.0
MASKED = -1e30

ATTN_COLS = [0, 1, 2, 3, 4, 5, 8, 9, 10, 11, 12, 13, 6, 7, 14, 15]
HEAD_OF = {"aq": 0, "ak": 4, "bq": 6, "bk": 10, "av": 12, "bv": 14}
N_ATTN_IN = 16
S_ATTN_OUT = N_ATTN_IN
S_FFN0 = S_ATTN_OUT + KT
N_FFN = 2 * FT + KT * len(FF_GROUPS)
S_GLA = S_FFN0 + N_FFN
N_GLA_ALL = 1 + 4 + 8
N_GLA_LAT = 4 + 8
S_GLA_OUT = S_GLA + N_GLA_ALL + N_GLA_LAT
S_FFN1 = S_GLA_OUT + KT
N_SLABS = S_FFN1 + N_FFN

ADA_TILES = 48
SH1, SC1, G1, SH2, SC2, G2 = range(0, ADA_TILES, KT)
FIRST_PAIRS = [(first + 2 * m) // 2 for m in range(KT // 2) for first in (SH1, SC1)]

VEC_WIDTHS = [("cond", 2 * KT), ("ada_b", 2 * ADA_TILES), ("ln_g", 4 * KT), ("ln_b", 4 * KT),
              ("conv_w", 2 * CONV_W * 2 * FT), ("conv_b", 2 * 2 * FT), ("q_norm", 1), ("k_norm", 1),
              ("sink", N_HEADS), ("b_a", 2 * GLA_HEADS), ("head_norm", 2), ("eps", 1)]
VEC = {}
_at = 0
for _name, _w in VEC_WIDTHS:
    VEC[_name] = _at
    _at += _w
N_VEC = _at


def below(value, bound):
    return isinstance(value, int) and value < bound


def last_two(s):
    return isinstance(s, int) and s + 2 >= N_SLABS


class Order:

    def __init__(self, engine, sem):
        self.engine, self.sem, self.n, self.extra = engine, sem, 0, 0

    def mark(self, instruction):
        instruction.then_inc(self.sem, 1)
        self.n += 1
        return self.n + self.extra

    def wait(self, value=None):
        self.engine.wait_ge(self.sem, self.n + self.extra if value is None else value)

    def enter(self, i, per):
        self.extra, self.start, self.per = i * per, self.n, per

    def leave(self, count):
        assert self.n - self.start == self.per, (self.n - self.start, self.per)
        self.n, self.extra = self.start + self.per * count, 0


def trunk(nc, x_in, vec_in, slabs_in, ada_in, rope_in, band_in, eye_in, a2_in, level_in, out):
    ctx = ExitStack()
    with ctx:
        top = [(nc.sbuf_base + 31) // 32 * 32]

        def place(name, shape, dtype=FP32, at=None):
            size = 4
            for n in shape:
                size *= n
            where = top[0] if at is None else at
            if at is None:
                top[0] += (size + 31) // 32 * 32
            return nc.alloc_sbuf_tensor_at(name, [P, *shape], dtype, offset=where)

        h_res = place("h_res", [KT, TOK])
        x_at = top[0]
        x_hi = place("x_hi", [KT, TOK], FP32R)
        x_lo = place("x_lo", [KT, TOK], FP32R)
        hid_at = top[0]
        hid_hi = place("hid_hi", [KT, TOK], FP32R)
        hid_lo = place("hid_lo", [KT, TOK], FP32R)
        raw_at = top[0]
        raw = [place(f"raw{j}", [KT * P]) for j in range(4)]
        w_hi = [place(f"w_hi{j}", [KT * P], FP32R) for j in range(2)]
        w_lo = [place(f"w_lo{j}", [KT * P], FP32R) for j in range(2)]
        ada_at = top[0]
        ada_w = [place(f"ada_w{j}", [2, KT * P]) for j in range(2)]
        ada_w += [nc.alloc_sbuf_tensor_at(f"ada_w{j + 2}", [P, 2, KT * P], FP32, offset=hid_at + 8 * KT * P * j)
                  for j in range(6)]
        vec = place("vec", [N_VEC])
        mods = place("mods", [2, ADA_TILES, 2])
        cond = place("cond", [KT, 2])
        ada_sum_at = top[0]
        ada_sum = place("ada_sum", [2, 2, 2 * P])
        mean_w = place("mean_w", [P])
        ones = place("ones", [P])
        eye = place("eye", [P])
        sums_at = top[0]
        place("chunk_sums", [4 * GLA_HEADS * 6 + 16])
        fused = place("fused", [2, KT, 2])
        small = place("small", [4, 6])
        free_at = top[0]
        assert free_at < nc.sbuf_usable_end

        def scratch(at, *shapes, dtype=FP32):
            got = []
            for name, shape in shapes:
                size = 4
                for n in shape:
                    size *= n
                got.append(nc.alloc_sbuf_tensor_at(name, [P, *shape], dtype, offset=at))
                at += (size + 31) // 32 * 32
            assert at <= nc.sbuf_usable_end, (shapes, at, nc.sbuf_usable_end)
            return got, at

        [qkv], _ = scratch(hid_at, ("qkv", [N_ATTN_IN, TOK]))
        [rope, band, row, v_tok], attn_at = scratch(
            free_at, ("rope", [2, LAT]), ("band", [3 * P]), ("row", [8, 8]), ("v_tok", [TOK // P, 4 * P]))
        [head_r, probs, probs_t], _ = scratch(
            attn_at, ("head_r", [6, TOK // P]), ("probs", [2, TOK]), ("probs_t", [2, TOK]))
        [rope_c, rope_s], _ = scratch(attn_at + 160, ("rope_c", [2, LAT]), ("rope_s", [2, LAT]))
        [square_a], _ = scratch(free_at + 5888, ("square_a", [4, TOK]))
        [sum1, sum2, tmp, acc_g, acc_v, hid_f, sq_t], _ = scratch(
            free_at, ("sum1", [TOK]), ("sum2", [TOK]), ("tmp", [2, TOK]), ("acc_g", [TOK]), ("acc_v", [TOK]),
            ("hid_f", [TOK]), ("sq_t", [2, TOK]))
        [mod_t], _ = scratch(free_at + 2 * 4 * TOK, ("mod_t", [4, TOK]))
        [gla_v, cum], _ = scratch(hid_at, ("gla_v", [TOK // P, 8 * P]), ("cum", [2, GLA_HEADS, TOK]))
        [a2, restart], _ = scratch(ada_at, ("a2", [2, GLA_HEADS * P]), ("restart", [TOK]))
        [gla_g], _ = scratch(ada_at, ("gla_g", [KT, LAT]))
        [gla_k, gla_q], gla_at = scratch(free_at, ("gla_k", [GLA_HEADS, TOK]), ("gla_q", [GLA_HEADS, LAT]))
        [low, soft], _ = scratch(gla_at, ("low", [TOK]), ("soft", [2, TOK]))
        [clipped], _ = scratch(ada_sum_at, ("clipped", [TOK]))
        [v_turn], _ = scratch(gla_at + 4 * TOK, ("v_turn", [2, TOK]))
        level = nc.alloc_sbuf_tensor_at("level", [P, 2 * GLA_LEVELS, P], mybir.dt.uint8, offset=gla_at)
        [q_in, o_buf], _ = scratch(
            gla_at + 2 * GLA_LEVELS * P, ("q_in", [2, LAT]), ("o_buf", [2, LAT]))
        [k_out], _ = scratch(ada_sum_at, ("k_out", [TOK]))
        both_b = nc.alloc_sbuf_tensor_at("both_b", [P, 2, LAT], FP32, offset=raw_at + 3 * 4 * KT * P)
        k_tok = nc.alloc_sbuf_tensor_at("k_tok", [P, 5, P], FP32, offset=raw_at)
        [level_f], _ = scratch(gla_at + 2 * GLA_LEVELS * P, ("level_f", [2 * GLA_LEVELS, P]))
        [chunk_sum, decay], _ = scratch(sums_at, ("chunk_sum", [2, GLA_HEADS, 6]), ("decay", [2, GLA_HEADS, 6]))
        [o_hi2, o_lo2], at = scratch(x_at, ("o_hi2", [KT, LAT]), ("o_lo2", [KT, LAT]), dtype=FP32R)
        [pairs, fade, both_a, o_r], _ = scratch(
            at, ("pairs", [2, LAT]), ("fade", [4, LAT]), ("both_a", [1, LAT]), ("o_r", [LAT]))

        pm = [ctx.enter_context(nc.psum_tensor(f"pm{j}", [P, 1024], FP32)) for j in range(4)]

        names = ["split_hi", "split_lo", "slab_done", "psum_free", "ada_done", "ada_taken", "ada_sum_lat",
                 "ada_sum_ctx", "first_sum", "vec_in", "const_in", "cond_done", "ones_done", "x_ready",
                 "hid_ready", "act_seq", "dve_seq", "pool_seq", "out_done", "ssq_done", "squared", "normed",
                 "roped", "rope_p", "v_turned", "v_copied", "score_done", "shift_done", "exp_done",
                 "probs_done", "turned", "turn_copied", "pv_done", "pv_copied", "o_hi", "residual", "summed",
                 "stat_done", "h_ready", "mod_f", "x_hi_done", "centred", "std_done", "lin_done", "silu_done",
                 "acc_free", "hid_split", "a2_in", "level_in", "level_done", "low_done", "logit_done",
                 "abs_done", "log_done", "ld_done", "diff_done", "fade_done", "both_done", "gram_done",
                 "level_used", "q_diff", "q_exp", "q_done", "k_diff", "k_exp", "k_done", "k_turned",
                 "k_copied", "s_prod", "s_done", "decay_done", "o_done", "o_sq", "o_ssq", "o_spread",
                 "o_r_copied", "o_std", "o_rms", "o_scaled", "o_gated", "o_hi_done", "o_ready", "exp_sink",
                 "var_done", "std2", "less_mean", "mean_done", "rms_done", "spread", "r_done", "squared_h",
                 "added", "sink_done", "half_copied", "key_r"]
        sem = {n: ctx.enter_context(nc.semaphore(n)) for n in names}
        raw_in = [ctx.enter_context(nc.semaphore(f"raw_in{j}")) for j in range(4)]
        ada_in_sem = [ctx.enter_context(nc.semaphore(f"ada_in{j}")) for j in range(2)]
        x_loaded = [ctx.enter_context(nc.semaphore(f"x_loaded{j}")) for j in range(KT // 2)]
        ada_first = [ctx.enter_context(nc.semaphore(f"ada_first{j}")) for j in range(8)]
        block = ctx.enter_context(nc.Block())

        def unit_scale(u):
            if u["sink"] is not None:
                return ATTN_SCALE
            return head_r[:, u["q"], u["q0"] // P:u["q0"] // P + 1]

        def tile_of(n, tokens):
            return h_res[:, bass.ds(n, 1), 0:tokens].rearrange("p a b -> p (a b)")

        def square(h):
            return square_a[:, h % 4, :]

        def col(name, k=0, n=1):
            return vec[:, bass.ds(VEC[name] + k, n)]

        HALVES = ((0, LAT), (LAT, TOK))
        LEVELS = 1 + 2 * GLA_LEVELS
        SCAN = ((4, 5, 0, 1, 2), (5, 4, 3, 2, 1))
        STATE = ((3, 0, 1, 2, 3), (0, 3, 2, 1, 0))

        def state(z, c):
            return h_res[:, 4 * z + c, LAT:TOK]

        def ada_bank(buffer):
            return pm[2][:, 512 * (buffer % 2):512 * (buffer % 2) + 4]

        def spread_r(a, b):
            return pm[2][:, a:b]

        def spread_m(a, b):
            return pm[3][:, a:b]

        def state_sum(j):
            return (pm[1][:, 256 * j:256 * (j + 1)] if j < 4 else pm[3][:, 0:256])

        def both(m):
            return both_a[:, 0, :] if m % 3 == 2 else both_b[:, m % 3, :]

        def level_bank(n):
            return pm[0][:, 512 * (n % 2):512 * (n % 2) + LAT]

        def segments(b, z, h, src=None):
            m = 1 << b
            v = (cum[:, z, h, 0:LAT] if src is None else src).rearrange("p (n t) -> p n t", t=2 * m)
            mid = m - 1 if z == 0 else m
            return v[:, :, 0:m], v[:, :, m:2 * m], v[:, :, mid:mid + 1].to_broadcast([P, LAT // (2 * m), m])

        def chunks(v):
            return v.rearrange("p (n t) -> p n t", t=GLA_CHUNK)

        def pair_arrived(engine, n, count, buffer):
            engine.wait_ge(ada_in_sem[buffer], 16 * count)
            engine.wait_ge(sem["ada_done"], n - 1)

        @block.sync
        def _(sp):
            sp.dma_start(vec[:, :], vec_in).then_inc(sem["vec_in"], 16)

            def slab_load(s, slot):
                if not below(s, 4):
                    sp.wait_ge(sem["split_lo"], s - 3)
                sp.dma_start(raw[slot][:, :], slabs_in[s]).then_inc(raw_in[slot], 16)

            def ada_load(n, slot):
                sp.wait_ge(sem["ada_done"], n - 1)
                sp.dma_start(ada_w[slot][:, :, :].rearrange("p a b -> p (a b)"), ada_in[n]).then_inc(ada_in_sem[slot], 16)

            for m in range(KT // 2):
                for j in (2 * m + 1, 2 * m):
                    sp.dma_start(ada_w[j][:, :, :].rearrange("p a b -> p (a b)"), ada_in[FIRST_PAIRS[j]]).then_inc(
                        ada_first[j], 16)
                    if j % 2 == 1:
                        sp.dma_start(h_res[:, 2 * m:2 * m + 2, :], x_in[:, 2 * m:2 * m + 2, :]).then_inc(x_loaded[m], 16)
                slab_load(m, m)
            sp.dma_start(rope[:, :, :], rope_in).then_inc(sem["const_in"], 16)
            for u in range(4):
                slab_load(4 + u, u)
            for n in range(2):
                ada_load(8 + n, n)
            with sp.Fori(2, 4) as i:
                for u in range(4):
                    slab_load(4 * i + u, u)
                    if u % 2 == 0:
                        ada_load(2 * i + 6 + u // 2, u // 2)
            for u in range(4):
                slab_load(16 + u, u)
            sp.dma_start(eye[:, :], eye_in).then_inc(sem["const_in"], 16)
            sp.dma_start(band[:, :], band_in).then_inc(sem["const_in"], 16)
            ada_load(14, 0)
            for n in range(15, 22):
                sp.wait_ge(sem["ada_sum_ctx"], n - 8)
                ada_load(n, n % 2 if n > 20 else 0)
            slab_load(20, 0), slab_load(21, 1)
            ada_load(22, 0)
            slab_load(22, 2), slab_load(23, 3)
            ada_load(23, 1)
            with sp.Fori(0, 12) as i:
                for u in range(4):
                    slab_load(4 * i + u + S_FFN0, u)
                    if u % 2 == 0:
                        ada_load(2 * i + u // 2 + 24, u // 2)
            with sp.Fori(18, 23) as i:
                for u in range(4):
                    slab_load(4 * i + u, u)
            sp.wait_ge(sem["ada_done"], ADA_TILES)
            sp.dma_start(a2[0:2 * GLA_RANK, :, :], a2_in).then_inc(sem["a2_in"], 16)
            with sp.Fori(23, 29) as i:
                for u in range(4):
                    slab_load(4 * i + u, u)
            sp.wait_ge(sem["v_copied"], TOK // P + 8)
            sp.dma_start(level_f[:, :, :], level_in).then_inc(sem["level_in"], 16)
            for u in range(3):
                slab_load(4 * 29 + u, u)
            sp.wait_ge(sem["gram_done"], LEVELS * GLA_HEADS)
            slab_load(4 * 29 + 3, 3)
            sp.wait_ge(sem["s_prod"], 2 * GLA_HEADS)
            with sp.Fori(30, N_SLABS // 4) as i:
                for u in range(4):
                    slab_load(4 * i + u, u)
            slab_load(N_SLABS - 1, (N_SLABS - 1) % 4)
            for n in range(KT):
                sp.wait_ge(sem["h_ready"], 3 * KT + n + 1)
                sp.dma_start(out[:, n, :], h_res[:, n, 0:LAT]).then_inc(sem["out_done"], 16)
            sp.wait_ge(sem["out_done"], 16 * KT)

        @block.tensor
        def _(pe):
            def ada_bank_free(n):
                if not below(n, 2):
                    pe.wait_ge(sem["ada_taken"], n - 1)

            def ada_pair(n, slot, dst=None):
                pe.wait_ge(sem["ada_sum_lat"], n - 7)
                pe.wait_ge(sem["ada_sum_ctx"], n - 7)
                ada_bank_free(n)
                if dst is None:
                    dst = ada_bank(slot)
                for half in range(2):
                    for c in range(2):
                        last = pe.matmul(dst[:, 2 * half + c:2 * half + c + 1],
                                         ada_sum[:, slot, c, half * P:(half + 1) * P], ones[:, 0:1],
                                         start=True, stop=True)
                last.then_inc(sem["ada_done"], 1)

            def slab(base, i, u, hi, lo, tokens, tiles=KT, ready=None, value=0):
                s = base + u + i * 4
                slot, out_p = (base + u) % 2, pm[(base + u) % 2]
                pe.wait_ge(sem["split_lo"], s + 1)
                if not below(s, 2):
                    pe.wait_ge(sem["psum_free"], s - 1)
                for k in range(tiles):
                    if ready is not None:
                        pe.wait_ge(ready, value + k + 1)
                    ks = slice(k * P, (k + 1) * P)
                    for w, x in ((w_hi, hi), (w_hi, lo), (w_lo, hi)):
                        for a, b in HALVES if tokens == TOK else HALVES[:1]:
                            last = pe.matmul(out_p[:, a:b], w[slot][:, ks], x[:, k, a:b],
                                             start=(k == 0 and w is w_hi and x is hi),
                                             stop=(k == tiles - 1 and w is w_lo))
                last.then_inc(sem["slab_done"], 1)

            def first_slabs(base, hi, lo, tokens, tiles, before=None):
                for n, (k, ready, value) in enumerate(tiles):
                    if before is not None:
                        before(n)
                    if n == 0:
                        pe.wait_ge(sem["split_lo"], base + 2)
                        if base > 0:
                            pe.wait_ge(sem["psum_free"], base)
                    pe.wait_ge(ready, value)
                    ks = slice(k * P, (k + 1) * P)
                    for slot in (base % 2, (base + 1) % 2):
                        for w, x in ((w_hi, hi), (w_hi, lo), (w_lo, hi)):
                            for a, b in HALVES if tokens == TOK else HALVES[:1]:
                                last = pe.matmul(pm[slot][:, a:b], w[slot][:, ks], x[:, k, a:b],
                                                 start=(n == 0 and w is w_hi and x is hi),
                                                 stop=(n == KT - 1 and w is w_lo))
                        if n == KT - 1:
                            last.then_inc(sem["slab_done"], 1)

            def modulated(count):
                return [(k, sem["x_ready"], KT * count + k + 1) for k in range(KT)]

            def spread(dst, per_token):
                return pe.matmul(dst, per_token.to_broadcast([P, P]), eye[:, :], start=True, stop=True)

            def stats(c, tokens=TOK):
                pe.wait_ge(sem["added"], KT * (c + 1))
                if c < 2:
                    pe.wait_ge(sem["ada_taken"], 24 * (c + 1))
                pe.wait_ge(sem["summed"], KT * (c + 1))
                for j, part in ((0, sum1), (1, sum2)):
                    for t in range(tokens // P):
                        last = pe.matmul(pm[2][:, 6 * j + t:6 * j + t + 1], part[:, t * P:(t + 1) * P], mean_w[:, 0:1],
                                         start=True, stop=True)
                last.then_inc(sem["stat_done"], 1)
                for j, ready, where in ((0, sem["mean_done"], spread_m), (2, sem["r_done"], spread_r)):
                    pe.wait_ge(ready, c + 1)
                    for t in range(tokens // P):
                        last = spread(where(t * P, (t + 1) * P), small[:, j, t:t + 1])
                    last.then_inc(sem["spread"], 1)

            pe.wait_ge(sem["cond_done"], 1)


            def first_scale(m):
                pe.wait_ge(sem["first_sum"], m + 1)
                pe.wait_ge(sem["ones_done"], 2)
                ada_bank_free(2 * m + 1)
                for half in range(2):
                    for c in range(2):
                        last = pe.matmul(ada_bank(1)[:, 2 * half + c:2 * half + c + 1],
                                         ada_sum[:, m % 2, c, half * P:(half + 1) * P], ones[:, 0:1],
                                         start=True, stop=True)
                last.then_inc(sem["ada_done"], 1)

            def first_direct(n):
                pe.wait_ge(ada_first[n], 16)
                ada_bank_free(n)
                for half in range(2):
                    for k in range(KT):
                        last = pe.matmul(ada_bank(n)[:, 2 * half:2 * half + 2],
                                         ada_w[n][:, half, k * P:(k + 1) * P],
                                         cond[:, k, :], start=(k == 0), stop=(k == KT - 1))
                last.then_inc(sem["ada_done"], 1)

            def first_pairs(k):
                if k % 2 == 0:
                    for m in ((0, 1) if k == 0 else (k // 2 + 1,)):
                        if m < KT // 2:
                            first_direct(2 * m)
                            first_scale(m)

            first_slabs(0, x_hi, x_lo, TOK, modulated(0), before=first_pairs)

            def head_squares(h):
                pe.wait_ge(sem["squared"], h + 1)
                for t in range(TOK // P):
                    last = pe.matmul(pm[3][:, 6 * h + t:6 * h + t + 1], square(h)[:, t * P:(t + 1) * P], ones[:, 0:1],
                                     start=True, stop=True)
                last.then_inc(sem["ssq_done"], 1)

            for s in range(2, 8):
                slab(0, 0, s, x_hi, x_lo, TOK)
                if s in (5, 7):
                    ada_pair(8 + s // 6, s // 6)
                head_squares(s - 2)
            with pe.Fori(2, 4) as i:
                for u in range(4):
                    slab(0, i, u, x_hi, x_lo, TOK)
                    if u % 2 == 1:
                        ada_pair(2 * i + 6 + u // 2, u // 2)
            pe.wait_ge(sem["const_in"], 48)
            pe.wait_ge(sem["psum_free"], N_ATTN_IN)
            for t in range(TOK // P):
                if t >= 2:
                    pe.wait_ge(sem["v_copied"], t - 1)
                for f in range(4):
                    last = pe.transpose(pm[t % 2][:, f * P:(f + 1) * P],
                                        qkv[:, HEAD_OF["av"] + f, t * P:(t + 1) * P], eye[:, :])
                last.then_inc(sem["v_turned"], 1)
            pe.wait_ge(sem["rms_done"], 1)
            pe.wait_ge(sem["ada_taken"], 14)
            for h in range(N_KV):
                for t in range(TOK // P):
                    last = spread(pm[2 + h][:, t * P:(t + 1) * P], head_r[:, N_HEADS + h, t:t + 1])
                last.then_inc(sem["key_r"], 1)

            def scores(n):
                u = UNITS[n]
                if n == 0:
                    pe.wait_ge(sem["roped"], 12)
                    pe.wait_ge(sem["v_copied"], TOK // P)
                if n == UNITS_B:
                    pe.wait_ge(sem["normed"], N_KV)
                if n >= 2:
                    pe.wait_ge(sem["exp_done"], n - 1)
                if n in ADA_UNITS:
                    ada_pair(ADA_UNITS[n], ADA_UNITS[n] % 2, pm[n % 2][:, TOK:TOK + 4])
                q = qkv[:, u["q"], u["q0"]:u["q0"] + P]
                for at, a, b in u["spans"]:
                    last = pe.matmul(pm[n % 2][:, at:at + b - a], q, qkv[:, u["k"], a:b], start=True,
                                     stop=(u["band"] is None or at > 0))
                    if u["band"] is not None and at == 0:
                        for m in u["band"]:
                            last = pe.matmul(pm[n % 2][:, m[0]:m[0] + P], eye[:, :], band[:, m[1]:m[1] + P],
                                             start=False, stop=(m is u["band"][-1]))
                last.then_inc(sem["score_done"], 1)

            def wait_copied(n):
                pe.wait_ge(sem["turn_copied"], n)
                pe.wait_ge(sem["half_copied"], sum(len(x["tiles"]) > 4 for x in UNITS[:n]))

            def turn(n):
                u = UNITS[n]
                pe.wait_ge(sem["probs_done"], n + 1)
                if n == 0:
                    pe.wait_ge(sem["normed"], N_KV)
                else:
                    wait_copied(n)
                for j in range(len(u["tiles"])):
                    last = pe.transpose(pm[2][:, j * P:(j + 1) * P], probs[:, n % 2, j * P:(j + 1) * P], eye[:, :])
                last.then_inc(sem["turned"], 1)

            def weigh(n):
                u = UNITS[n]
                wait_copied(n + 1)
                if u["first"] and u["out"] >= 2:
                    pe.wait_ge(sem["pv_copied"], u["out"] - 1)
                at = 512 * (u["out"] % 2) + u["o0"]
                for j, t in enumerate(u["tiles"]):
                    last = pe.matmul(pm[3][:, at:at + P], v_tok[:, t, u["v"] * P:(u["v"] + 1) * P],
                                     probs_t[:, n % 2, j * P:(j + 1) * P], start=(j == 0), stop=(j == len(u["tiles"]) - 1))
                if u["last"]:
                    last.then_inc(sem["pv_done"], 1)

            scores(0)
            scores(1)
            for n in range(len(UNITS)):
                if n + 2 < len(UNITS):
                    scores(n + 2)
                if n >= 1:
                    weigh(n - 1)
                turn(n)

            def last_unit(n):
                if n == 3:
                    weigh(len(UNITS) - 1)

            outs = [(k, sem["pv_copied"], o + 1) for o, (k, a, b) in enumerate(OUTS) if b == TOK]
            first_slabs(S_ATTN_OUT, x_hi, x_lo, TOK, outs, before=last_unit)
            for u in range(1, KT):
                if u >= 2:
                    slab(S_ATTN_OUT, 0, u, x_hi, x_lo, TOK)
                if u in PAIR_AFTER:
                    ada_pair(PAIR_AFTER[u], PAIR_AFTER[u] % 2)
            stats(0)

            def ffn(base, layer, tokens):
                s = base
                for g, tiles in enumerate(FF_GROUPS):
                    def beside(i, u):
                        if layer == 0 and g < 2 and u % 2 == 1:
                            ada_pair(24 + (s - S_FFN0) // 2 + 2 * i + u // 2, u // 2)

                    if g == 0:
                        first_slabs(s, x_hi, x_lo, tokens, modulated(1 + 2 * layer))
                        beside(0, 1)
                        for u in range(2, 4):
                            slab(s, 0, u, x_hi, x_lo, tokens)
                            beside(0, u)
                    with pe.Fori(1 if g == 0 else 0, tiles // 2) as i:
                        for u in range(4):
                            slab(s, i, u, x_hi, x_lo, tokens)
                            beside(i, u)
                    s += 2 * tiles
                    with pe.Fori(0, 2) as i:
                        for u in range(4):
                            slab(s, i, u, hid_hi, hid_lo, tokens, tiles, ready=sem["hid_ready"] if u == 0 else None,
                                 value=FT * layer + sum(FF_GROUPS[:g]))
                            beside(i, u)
                    s += KT

            ffn(S_FFN0, 0, TOK)
            stats(1)

            def logits(j):
                z, h = j // GLA_HEADS, j % GLA_HEADS
                if j == 0:
                    pe.wait_ge(sem["low_done"], 1)
                    pe.wait_ge(sem["a2_in"], 16)
                    pe.wait_ge(sem["h_ready"], 2 * KT)
                if j >= 2:
                    pe.wait_ge(sem["ld_done"], j - 1)
                for a, b in HALVES:
                    last = pe.matmul(pm[2 + j % 2][:, a:b], a2[0:2 * GLA_RANK, z, h * P:(h + 1) * P],
                                     low[0:2 * GLA_RANK, a:b], start=True, stop=True)
                last.then_inc(sem["logit_done"], 1)

            first_slabs(S_GLA, x_hi, x_lo, TOK, modulated(2))
            for n in range(GLA_HEADS):
                if n >= 1:
                    slab(S_GLA, 0, n + 1, x_hi, x_lo, TOK)
                logits(2 * n)
                logits(2 * n + 1)
            s_v = S_GLA + 1 + GLA_HEADS
            with pe.Fori(0, 2) as i:
                def turn_v(u):
                    pe.wait_ge(sem["psum_free"], s_v + u + 1 + 4 * i)
                    pe.wait_ge(sem["v_copied"], TOK // P + u - 1 + 4 * i)
                    for t in range(TOK // P):
                        last = pe.transpose(pm[2 + u % 2][:, t * P:(t + 1) * P], v_turn[:, u % 2, t * P:(t + 1) * P],
                                            eye[:, :])
                    last.then_inc(sem["v_turned"], 1)

                for u in range(4):
                    slab(s_v, i, u, x_hi, x_lo, TOK)
                    if u >= 1:
                        turn_v(u - 1)
                turn_v(3)
            with pe.Fori(0, 3) as i:
                for u in range(4):
                    slab(S_GLA + N_GLA_ALL, i, u, x_hi, x_lo, LAT)

            pe.wait_ge(sem["psum_free"], S_GLA_OUT)
            pe.wait_ge(sem["v_copied"], TOK // P + 8)

            def turn_keys(q):
                pe.wait_ge(sem["k_done"], q + 1)
                if q >= 1:
                    pe.wait_ge(sem["k_copied"], q)
                for j, c in enumerate(SCAN[q % 2]):
                    last = pe.transpose(pm[2][:, j * P:(j + 1) * P], k_out[:, c * P:(c + 1) * P], eye[:, :])
                last.then_inc(sem["k_turned"], 1)

            def chunk_states(q):
                h = q // 2
                pe.wait_ge(sem["k_copied"], q + 1)
                if q >= 1:
                    pe.wait_ge(sem["s_done"], 5 * q)
                if h >= 1:
                    pe.wait_ge(sem["o_scaled"], 2 * h)
                for j, c in enumerate(SCAN[q % 2]):
                    last = pe.matmul(state_sum(j), k_tok[:, j, :], gla_v[:, c, 2 * h * P:2 * (h + 1) * P],
                                     start=True, stop=True)
                last.then_inc(sem["s_prod"], 1)

            def gram(h, lv):
                n = LEVELS * h + lv
                if n >= 2:
                    pe.wait_ge(sem["level_used"], n - 1)
                if lv > 0:
                    m = (LEVELS - 1) * h + lv - 1
                    pe.wait_ge(sem["both_done"], m + 1)
                    lhs, rhs = both(m), both(m)
                else:
                    lhs, rhs = gla_k[:, h, :], gla_q[:, h, :]
                for c in range(4):
                    cs = slice(c * P, (c + 1) * P)
                    last = pe.matmul(level_bank(n)[:, cs], lhs[:, cs], rhs[:, cs], start=True, stop=True)
                last.then_inc(sem["gram_done"], 1)

            def head_output(h, pieces=range(4)):
                if 0 in pieces:
                    pe.wait_ge(sem["level_used"], LEVELS * (h + 1))
                    pe.wait_ge(sem["q_done"], h + 1)
                    pe.wait_ge(sem["s_done"], 10 * (h + 1))
                for piece in pieces:
                    vt = piece // 2
                    v0 = (2 * h + vt) * P
                    for c in (2 * (piece % 2), 2 * (piece % 2) + 1):
                        dst = pm[3][:, 512 * vt + c * P:512 * vt + (c + 1) * P]
                        cs = slice(c * P, (c + 1) * P)
                        pe.matmul(dst, gla_v[:, c, v0:v0 + P], pairs[:, h % 2, cs], start=True, stop=False)
                        pe.matmul(dst, state(0, c)[:, vt * P:(vt + 1) * P], q_in[:, 0, cs], start=False, stop=False)
                        last = pe.matmul(dst, state(1, c)[:, vt * P:(vt + 1) * P], q_in[:, 1, cs], start=False, stop=True)
                if 3 in pieces:
                    last.then_inc(sem["o_done"], 1)

            def head_sums(h):
                pe.wait_ge(sem["o_sq"], 2 * (h + 1))
                for t in range(LAT // P):
                    for vt in range(2):
                        last = pe.matmul(pm[1][:, 512 + t:513 + t], o_buf[:, vt, t * P:(t + 1) * P], ones[:, 0:1],
                                         start=(vt == 0), stop=(vt == 1))
                last.then_inc(sem["o_ssq"], 1)

            def head_spread(h):
                pe.wait_ge(sem["o_rms"], h + 1)
                for t in range(LAT // P):
                    last = spread(pm[1][:, 512 + t * P:512 + (t + 1) * P], small[:, 3, t:t + 1])
                last.then_inc(sem["o_spread"], 1)

            for h in range(GLA_HEADS):
                for lv in range(LEVELS):
                    gram(h, lv)
                    if h >= 1 and lv in (1, 2, 3, 4):
                        head_output(h - 1, (lv - 1,))
                    if lv == 5:
                        turn_keys(2 * h)
                    if h >= 1 and lv == 7:
                        head_sums(h - 1)
                    if h >= 1 and lv == 8:
                        head_spread(h - 1)
                    if lv == 10:
                        chunk_states(2 * h)
                    if lv == 11:
                        turn_keys(2 * h + 1)
                    if lv == 13:
                        chunk_states(2 * h + 1)
            head_output(GLA_HEADS - 1)

            def last_head(k):
                if k == 3:
                    head_sums(GLA_HEADS - 1)
                if k == 6:
                    head_spread(GLA_HEADS - 1)

            first_slabs(S_GLA_OUT, o_hi2, o_lo2, LAT, [(k, sem["o_ready"], k + 1) for k in range(KT)],
                        before=last_head)
            for u in range(2, KT):
                slab(S_GLA_OUT, 0, u, o_hi2, o_lo2, LAT)
            stats(2, LAT)
            ffn(S_FFN1, 1, LAT)
            stats(3, LAT)

        @block.scalar
        def _(act):
            order = Order(act, sem["act_seq"])

            def split(s, slot):
                act.wait_ge(raw_in[slot % 4], 16)
                act.activation(w_hi[slot % 2][:, :], raw[slot % 4][:, :], ACT.Copy).then_inc(sem["split_hi"], 1)

            def step(base, i, u, evacuate, first=False):
                s = base + u + 4 * i
                act.wait_ge(sem["slab_done"], s + 1)
                if first:
                    evacuate(s, i, u, pm[(base + u) % 2])
                nxt = base + u + 2
                if not last_two(s):
                    act.wait_ge(raw_in[nxt % 4], 16 * (nxt // 4 + 1) + 16 * i)
                    act.activation(w_hi[nxt % 2][:, :], raw[nxt % 4][:, :], ACT.Copy).then_inc(sem["split_hi"], 1)
                if not first:
                    evacuate(s, i, u, pm[(base + u) % 2])

            act.wait_ge(sem["vec_in"], 16)
            act.activation(cond[:, :, :].rearrange("p a b -> p (a b)"), col("cond", 0, 2 * KT), ACT.Silu).then_inc(
                sem["cond_done"], 1)

            def modulate(n, first, tokens, scale, shift):
                act.wait_ge(sem["x_ready"], first + n - 3)
                for c, (a, b) in enumerate(HALVES if tokens == TOK else HALVES[:1]):
                    last = act.activation(mod_t[:, n % 4, a:b], h_res[:, n, a:b], ACT.Identity,
                                          bias=shift[:, n, c:c + 1], scale=scale[:, n, c:c + 1])
                last.then_inc(sem["mod_f"], 1)

            def high_part(n, first, tokens):
                act.wait_ge(sem["mod_f"], first + n + 1)
                act.activation(x_hi[:, n, 0:tokens], mod_t[:, n % 4, 0:tokens], ACT.Copy).then_inc(sem["x_hi_done"], 1)

            for n in range(KT):
                high_part(n, 0, TOK)
                if n == 1:
                    for s in range(2):
                        split(s, s)

            def copy_qkv(s, i, u, src):
                act.activation(qkv[:, s, :], src[:, 0:TOK], ACT.Copy).then_inc(sem["psum_free"], 1)

            with act.Fori(0, 4) as i:
                for u in range(4):
                    step(0, i, u, copy_qkv)

            act.wait_ge(sem["ssq_done"], 6)
            act.activation(head_r[:, :, :].rearrange("p a b -> p (a b)"), pm[3][:, 0:36], ACT.Sqrt, bias=col("eps"),
                           scale=1.0 / HEAD_DIM).then_inc(sem["std_done"], 1)
            for t in range(TOK // P):
                act.wait_ge(sem["v_turned"], t + 1)
                act.activation(v_tok[:, t, :], pm[t % 2][:, 0:4 * P], ACT.Copy).then_inc(sem["v_copied"], 1)

            def half_turn(n):
                width = min(len(UNITS[n]["tiles"]), 4) * P
                act.wait_ge(sem["turned"], n + 1)
                act.activation(probs_t[:, n % 2, 0:width], pm[2][:, 0:width], ACT.Copy).then_inc(sem["turn_copied"], 1)

            def out_hi(o):
                act.wait_ge(sem["pv_done"], o + 1)
                k, a, b = OUTS[o]
                at = 512 * (o % 2)
                act.activation(x_hi[:, k, a:b], pm[3][:, at:at + b - a], ACT.Copy).then_inc(sem["o_hi"], 1)

            def exponentiate(n):
                u = UNITS[n]
                act.wait_ge(sem["shift_done"], n + 1)
                if n >= 2:
                    act.wait_ge(sem["turned"], n - 1)
                width = len(u["tiles"]) * P
                src = pm[n % 2][:, 0:width]
                r = row[:, n % 8, :]
                act.activation(probs[:, n % 2, 0:width], src, ACT.Exp, bias=r[:, 1:2], scale=unit_scale(u),
                               accum_out=r[:, 2:3]).then_inc(sem["exp_done"], 1)
                if u["sink"] is not None:
                    act.activation(r[:, 3:4], col("sink", u["sink"]), ACT.Exp, bias=r[:, 1:2], scale=-1.0).then_inc(
                        sem["exp_sink"], 1)

            for n in range(len(UNITS) + 1):
                if n < len(UNITS):
                    exponentiate(n)
                if n >= 1:
                    half_turn(n - 1)
                if n >= 2 and UNITS[n - 2]["last"]:
                    out_hi(UNITS[n - 2]["out"])
            out_hi(len(OUTS) - 1)

            first_res = [0]

            def residual_phase(base, layer, part, tokens, norm=None):
                act.wait_ge(sem["ada_taken"], 12 if base == S_ATTN_OUT else 24 * (layer + 1))

                def evacuate(s, i, u, src):
                    n = i * 4 + u
                    done = first_res[0] + n - 1
                    if not below(done, 1):
                        act.wait_ge(sem["residual"], done)
                    halves = HALVES if tokens == TOK else HALVES[:1]
                    for c, (a, b) in enumerate(halves):
                        last = act.activation(tmp[:, u % 2, a:b], src[:, a:b], ACT.Copy,
                                              scale=mods[:, layer, bass.ds(part + n, 1), c])
                    last.then_inc(sem["psum_free"], 1)
                    if norm is not None:
                        if not (norm == 0 and below(n, 2)):
                            act.wait_ge(sem["summed"], KT * norm + n - 1)
                        act.wait_ge(sem["residual"], first_res[0] + n + 1)
                        act.activation(sq_t[:, u % 2, 0:tokens], tile_of(n, tokens), ACT.Square).then_inc(
                            sem["squared_h"], 1)
                if first_res[0] == 0 or base + KT == N_SLABS:
                    for j in range(8):
                        step(base + j, 0, 0, lambda s, i, u, src, j=j: evacuate(s, 0, j, src), first=j == 7)
                else:
                    with act.Fori(0, 2) as i:
                        for u in range(4):
                            step(base, i, u, evacuate, first=norm is not None and u == 3)
                first_res[0] += KT

            def norm_phase(c, tokens):
                act.wait_ge(sem["var_done"], c + 1)
                n = tokens // P
                act.activation(small[:, 2, 0:n], small[:, 1, 0:n], ACT.Sqrt, bias=col("eps")).then_inc(sem["std2"], 1)
                if c == 3:
                    for n in range(KT):
                        act.wait_ge(sem["centred"], KT * c + n + 1)
                        act.activation(h_res[:, n, 0:tokens], h_res[:, n, 0:tokens], ACT.Identity,
                                       bias=col("ln_b", KT * c + n), scale=col("ln_g", KT * c + n)).then_inc(sem["h_ready"], 1)
                    return
                for n in range(KT + 1):
                    if n < KT:
                        act.wait_ge(sem["centred"], KT * c + n + 1)
                        modulate(n, KT * (c + 1), tokens, fused[:, 0, :, :], fused[:, 1, :, :])
                    if n == 0 or n >= 2:
                        high_part(max(n - 1, 0), KT * (c + 1), tokens)

            residual_phase(S_ATTN_OUT, 0, G1, TOK, norm=0)
            norm_phase(0, TOK)
            def ffn(base, layer, tokens):
                s0 = base
                done = FT * layer
                for g, tiles in enumerate(FF_GROUPS):
                    with act.Fori(0, tiles // 2) as i:
                        for u in range(4):
                            def evacuate(s, i, u, src):
                                j = sum(FF_GROUPS[:g]) + 2 * i + u // 2
                                tile = j + FT * (u % 2)
                                pair = done + 2 * i + u // 2
                                acc = (acc_g, acc_v)[u % 2]
                                act.wait_ge(sem["acc_free"], pair + 1)
                                act.activation(acc[:, 0:tokens], src[:, 0:tokens], ACT.Identity,
                                               bias=vec[:, bass.ds(VEC["conv_b"] + 2 * FT * layer + tile, 1)],
                                               scale=vec[:, bass.ds(VEC["conv_w"] + 2 * FT * (CONV_W * layer + 1) + tile, 1)]
                                               ).then_inc(sem["lin_done"], 1)
                                if u % 2 == 1:
                                    act.wait_ge(sem["psum_free"], s)
                                    act.activation(acc_g[:, 0:tokens], acc_g[:, 0:tokens], ACT.Silu).then_inc(
                                        sem["silu_done"], 1)
                                    act.wait_ge(sem["acc_free"], pair + 2)
                                    act.activation(hid_hi[:, bass.ds(2 * i + u // 2, 1), 0:tokens],
                                                   hid_f[:, 0:tokens].rearrange("p (a b) -> p a b", a=1), ACT.Copy).then_inc(sem["hid_split"], 1)
                            step(s0, i, u, evacuate)
                    done += tiles
                    s0 += 2 * tiles
                    residual_phase(s0, layer, G2, tokens, norm=None if g < 2 else 1 + 2 * layer)
                    s0 += KT

            ffn(S_FFN0, 0, TOK)
            norm_phase(1, TOK)

            def take_low(s, i, u, src):
                act.activation(low[0:2 * GLA_RANK, :], src[0:2 * GLA_RANK, 0:TOK], ACT.Copy).then_inc(sem["psum_free"], 1)
                act.wait_ge(sem["psum_free"], s + 1)
                act.sem_inc(sem["low_done"], 1)

            def take_key(s, i, u, src):
                act.activation(gla_k[:, u - 1, :], src[:, 0:TOK], ACT.Copy).then_inc(sem["psum_free"], 1)

            def softplus(h):
                both_ways = (2 * h, 2 * h + 1)
                for j in both_ways:
                    act.wait_ge(sem["logit_done"], j + 1)
                    if j >= 2:
                        act.wait_ge(sem["ld_done"], j - 1)
                    act.activation(soft[:, j % 2, :], pm[2 + j % 2][:, 0:TOK], ACT.Abs, bias=col("b_a", j)).then_inc(
                        sem["abs_done"], 1)
                for j in both_ways:
                    act.wait_ge(sem["abs_done"], j + 1)
                    order.mark(act.activation(soft[:, j % 2, :], soft[:, j % 2, :], ACT.Exp, scale=-1.0))
                order.wait()
                for j in both_ways:
                    act.activation(soft[:, j % 2, :], soft[:, j % 2, :], ACT.Ln, bias=1.0).then_inc(sem["log_done"], 1)

            step(S_GLA, 0, 0, take_low)
            for n in range(GLA_HEADS):
                step(S_GLA, 0, n + 1, take_key)
                softplus(n)
            act.wait_ge(sem["ld_done"], 2 * GLA_HEADS)
            with act.Fori(0, 2) as i:
                def take_value(s, i, u, src):
                    act.wait_ge(sem["v_turned"], TOK // P + u - 1 + 4 * i)
                    act.activation(v_turn[:, u % 2, :], src[:, 0:TOK], ACT.Copy).then_inc(sem["psum_free"], 1)

                def copy_value(u):
                    act.wait_ge(sem["v_turned"], TOK // P + u + 1 + 4 * i)
                    act.activation(gla_v[:, :, bass.ds(4 * P * i + u * P, P)],
                                   pm[2 + u % 2][:, 0:TOK].rearrange("p (a b) -> p a b", b=P), ACT.Copy).then_inc(
                        sem["v_copied"], 1)

                for u in range(4):
                    step(S_GLA + 1 + GLA_HEADS, i, u, take_value)
                    if u >= 1:
                        copy_value(u - 1)
                copy_value(3)

            def take_query(s, i, u, src):
                act.activation(gla_q[:, u, :], src[:, 0:LAT], ACT.Copy, scale=P ** -0.5).then_inc(sem["psum_free"], 1)

            def take_gate(s, i, u, src):
                act.activation(gla_g[:, bass.ds(4 * i + u, 1), :], src[:, 0:LAT].rearrange("p (a b) -> p a b", a=1),
                               ACT.Silu).then_inc(sem["psum_free"], 1)

            for u in range(4):
                step(S_GLA + N_GLA_ALL, 0, u, take_query)
            with act.Fori(0, 2) as i:
                for u in range(4):
                    step(S_GLA + N_GLA_ALL + 4, i, u, take_gate)

            INV = 1.0 / 16.0
            act.activation(decay[:, :, :, :].rearrange("p a b c -> p (a b c)"),
                           chunk_sum[:, :, :, :].rearrange("p a b c -> p (a b c)"), ACT.Exp, scale=INV).then_inc(
                sem["decay_done"], 1)
            act.wait_ge(sem["slab_done"], S_GLA_OUT)

            def key_decay(q):
                h = q // 2
                if q % 2 == 0:
                    act.wait_ge(sem["k_diff"], h + 1)
                    src = k_out[:, :]
                else:
                    act.wait_ge(sem["k_turned"], q)
                    src = cum[:, 1, h, :]
                act.activation(k_out[:, :], src, ACT.Exp, scale=INV).then_inc(sem["k_exp"], 1)

            def copy_keys(q):
                act.wait_ge(sem["k_turned"], q + 1)
                if q == 0:
                    act.wait_ge(sem["split_lo"], S_GLA_OUT)
                else:
                    act.wait_ge(sem["s_prod"], q)
                act.activation(k_tok[:, :, :], pm[2][:, 0:5 * P].rearrange("p (a b) -> p a b", b=P), ACT.Copy).then_inc(
                    sem["k_copied"], 1)

            def query_decay(h):
                act.wait_ge(sem["q_diff"], h + 1)
                act.activation(q_in[:, 0, :], cum[:, 0, h, 0:LAT], ACT.Exp, scale=INV)
                act.activation(q_in[:, 1, :], q_in[:, 1, :], ACT.Exp, scale=INV).then_inc(sem["q_exp"], 1)

            def diagonal(h):
                n = LEVELS * h
                act.wait_ge(sem["gram_done"], n + 1)
                if h >= 1:
                    act.wait_ge(sem["level_used"], n)
                if h >= 2:
                    act.wait_ge(sem["o_done"], h - 1)
                act.activation(pairs[:, h % 2, :], level_bank(n), ACT.Copy, scale=2.0).then_inc(sem["level_used"], 1)

            def square_output(h):
                act.wait_ge(sem["o_done"], h + 1)
                if h >= 1:
                    act.wait_ge(sem["o_ready"], 2 * h)
                for vt in range(2):
                    act.activation(o_buf[:, vt, :], pm[3][:, 512 * vt:512 * (vt + 1)], ACT.Square).then_inc(sem["o_sq"], 1)

            def output_std(h):
                act.wait_ge(sem["o_ssq"], h + 1)
                act.activation(small[:, 2, 0:4], pm[1][:, 512:516], ACT.Sqrt, bias=col("eps"), scale=1.0 / (2 * P)).then_inc(
                    sem["o_std"], 1)

            def copy_rms(h):
                act.wait_ge(sem["o_spread"], h + 1)
                if h >= 1:
                    act.wait_ge(sem["o_scaled"], 2 * h)
                act.activation(o_r[:, :], pm[1][:, 512:1024], ACT.Copy).then_inc(sem["o_r_copied"], 1)

            def finish_head(h):
                for vt in range(2):
                    act.wait_ge(sem["o_gated"], 2 * h + vt + 1)
                    act.activation(o_hi2[:, 2 * h + vt, :], o_buf[:, vt, :], ACT.Copy).then_inc(sem["o_hi_done"], 1)

            key_decay(0)
            for h in range(GLA_HEADS):
                for lv in range(LEVELS - 1):
                    m = (LEVELS - 1) * h + lv
                    act.wait_ge(sem["diff_done"], m + 1)
                    act.activation(fade[:, m % 4, :], fade[:, m % 4, :], ACT.Exp, scale=INV).then_inc(sem["fade_done"], 1)
                    if lv == 1:
                        diagonal(h)
                    if h >= 1 and lv == 6:
                        square_output(h - 1)
                    if lv == 7:
                        copy_keys(2 * h)
                        key_decay(2 * h + 1)
                    if h >= 1 and lv == 8:
                        output_std(h - 1)
                    if h >= 1 and lv == 9:
                        copy_rms(h - 1)
                    if lv == 10:
                        query_decay(h)
                    if lv == 12:
                        copy_keys(2 * h + 1)
                if h + 1 < GLA_HEADS:
                    key_decay(2 * h + 2)
                if h >= 1:
                    finish_head(h - 1)
            square_output(GLA_HEADS - 1)
            output_std(GLA_HEADS - 1)
            copy_rms(GLA_HEADS - 1)
            finish_head(GLA_HEADS - 1)

            residual_phase(S_GLA_OUT, 1, G1, LAT, norm=2)
            norm_phase(2, LAT)
            ffn(S_FFN1, 1, LAT)
            norm_phase(3, LAT)

        @block.vector
        def _(dve):
            order = Order(dve, sem["dve_seq"])

            def rest(s, nxt, i=0):
                dve.wait_ge(sem["split_hi"], s + 1)
                dve.tensor_tensor(w_lo[nxt % 2][:, :], raw[nxt % 4][:, :], w_hi[nxt % 2][:, :].bitcast(FP32),
                                  ALU.subtract).then_inc(sem["split_lo"], 1)

            def step(base, i, u, evacuate=None, first=False):
                s = base + u + 4 * i
                if first:
                    evacuate(s, i, u, pm[(base + u) % 2])
                if not last_two(s):
                    rest(s + 2, base + u + 2)
                if evacuate is not None and not first:
                    evacuate(s, i, u, pm[(base + u) % 2])

            dve.memset(mean_w[:, :], 1.0 / D_MODEL).then_inc(sem["ones_done"], 1)
            dve.memset(ones[:, :], 1.0).then_inc(sem["ones_done"], 1)
            dve.memset(acc_g[:, 0:1], 0.0).then_inc(sem["acc_free"], 1)

            def add_up(weights, c, slot):
                total = ada_sum[:, slot, c, :].rearrange("p (a b) -> p a b", a=2)
                for k in range(KT):
                    w = weights[:, :, k * P:(k + 1) * P]
                    if k == 0:
                        last = dve.tensor_scalar(total, w, cond[:, k, c:c + 1], None, ALU.mult)
                    else:
                        last = dve.scalar_tensor_tensor(total, w, cond[:, k, c:c + 1], total, ALU.mult, ALU.add)
                    if k < KT - 1:
                        order.mark(last)
                        order.wait()
                return last

            def add_pair(n, count, buffer):
                pair_arrived(dve, n, count, buffer)
                add_up(ada_w[buffer], 0, buffer).then_inc(sem["ada_sum_lat"], 1)

            def take_pair(n, layer, first, buffer, scale=False, src=None):
                dve.wait_ge(sem["ada_done"], n + 1)
                got = mods[:, layer, bass.ds(first, 2), :]
                src = (ada_bank(buffer) if src is None else src).rearrange("p (a b) -> p a b", b=2)
                bias = col("ada_b", first + ADA_TILES * layer, 2).unsqueeze(2).to_broadcast([P, 2, 2])
                dve.scalar_tensor_tensor(got, src, 1.0 if scale else 0.0, bias, ALU.add, ALU.add).then_inc(
                    sem["ada_taken"], 1)

            dve.wait_ge(sem["vec_in"], 16)
            dve.tensor_scalar(col("sink", 0, N_HEADS), col("sink", 0, N_HEADS), -1.0, None, ALU.mult).then_inc(
                sem["sink_done"], 1)
            dve.wait_ge(sem["cond_done"], 1)
            for n in range(KT):
                if n % 2 == 0:
                    m = n // 2
                    dve.wait_ge(ada_first[2 * m + 1], 16)
                    if m >= 2:
                        dve.wait_ge(sem["ada_done"], 2 * m - 2)
                    order.mark(add_up(ada_w[2 * m + 1], 0, m % 2))
                    add_up(ada_w[2 * m + 1], 1, m % 2).then_inc(sem["first_sum"], 1)
                    if m == 1:
                        for s in range(2):
                            rest(s, s)
                take_pair(n, 0, 2 * FIRST_PAIRS[n], n, scale=n % 2 == 1)
                if n % 2 == 1:
                    dve.wait_ge(sem["ada_taken"], n + 1)
                    dve.wait_ge(x_loaded[n // 2], 16)
                    for m in (n - 1, n):
                        if m >= 4:
                            dve.wait_ge(sem["x_ready"], m - 3)
                        for c, (a, b) in enumerate(HALVES):
                            last = dve.tensor_scalar(mod_t[:, m % 4, a:b], h_res[:, m, a:b], mods[:, 0, SC1 + m, c:c + 1],
                                                     mods[:, 0, SH1 + m, c:c + 1], ALU.mult, ALU.add)
                        last.then_inc(sem["mod_f"], 1)

            def rotate(h):
                z = qkv[:, h, 0:LAT]
                b = h % 2
                dve.wait_ge(sem["psum_free"], h + 1)
                if h >= 2:
                    dve.wait_ge(sem["roped"], h - 1)
                if h < 6:
                    g = col("q_norm") if h < N_HEADS else col("k_norm")
                    dve.scalar_tensor_tensor(rope_s[0:64, b, :], z[64:128, :], g[64:128, :], rope[64:128, 1, :],
                                             ALU.mult, ALU.mult)
                    dve.scalar_tensor_tensor(rope_s[64:128, b, :], z[0:64, :], g[0:64, :], rope[0:64, 1, :],
                                             ALU.mult, ALU.mult)
                    dve.scalar_tensor_tensor(rope_c[:, b, :], z, g, rope[:, 0, :], ALU.mult, ALU.mult).then_inc(
                        sem["rope_p"], 1)
                    dve.wait_ge(sem["squared"], h + 1)
                    order.mark(dve.tensor_scalar(qkv[:, h, LAT:TOK], qkv[:, h, LAT:TOK], g, None, ALU.mult))
                else:
                    dve.tensor_tensor(rope_s[0:64, b, :], z[64:128, :], rope[64:128, 1, :], ALU.mult)
                    dve.tensor_tensor(rope_s[64:128, b, :], z[0:64, :], rope[0:64, 1, :], ALU.mult)
                    dve.tensor_tensor(rope_c[:, b, :], z, rope[:, 0, :], ALU.mult).then_inc(sem["rope_p"], 1)
                dve.wait_ge(sem["rope_p"], h + 1)
                dve.tensor_tensor(z, rope_c[:, b, :], rope_s[:, b, :], ALU.add).then_inc(sem["roped"], 1)

            for s in range(N_ATTN_IN):
                step(0, 0, s)
                if s == 1:
                    dve.wait_ge(sem["const_in"], 16)
                if 1 <= s <= 12:
                    rotate(s - 1)
                n = 8 + (s - 3) // 2
                if s >= 5 and s % 2 == 1:
                    take_pair(n - 1, 0, 2 * (n - 1), n - 1)
                if 3 <= s <= 13 and s % 2 == 1:
                    add_pair(n, (s - 3) // 4 + 1, n % 2)
            dve.wait_ge(sem["std_done"], 1)
            order.mark(dve.reciprocal(head_r[:, :, :], head_r[:, :, :]))
            order.wait()
            dve.tensor_scalar(head_r[:, 0:N_HEADS, :], head_r[:, 0:N_HEADS, :], ATTN_SCALE, None, ALU.mult).then_inc(
                sem["rms_done"], 1)
            for h in range(N_KV):
                dve.wait_ge(sem["key_r"], h + 1)
                k = qkv[:, HEAD_OF["ak"] + h, :]
                if h == 0:
                    dve.wait_ge(sem["roped"], 12)
                dve.tensor_tensor(k, k, pm[2 + h][:, 0:TOK], ALU.mult).then_inc(sem["normed"], 1)

            def out_lo(o):
                k, a, b = OUTS[o]
                at = 512 * (o % 2)
                dve.wait_ge(sem["o_hi"], o + 1)
                dve.tensor_tensor(x_lo[:, k, a:b], pm[3][:, at:at + b - a], x_hi[:, k, a:b].bitcast(FP32),
                                  ALU.subtract).then_inc(sem["pv_copied"], 1)

            def copy_turned(n):
                width = len(UNITS[n]["tiles"]) * P
                if width > 4 * P:
                    dve.wait_ge(sem["turned"], n + 1)
                    dve.tensor_copy(probs_t[:, n % 2, 4 * P:width], pm[2][:, 4 * P:width]).then_inc(sem["half_copied"], 1)

            def shift(n):
                u = UNITS[n]
                width = len(u["tiles"]) * P
                r = row[:, n % 8, :]
                dve.wait_ge(sem["score_done"], n + 1)
                order.mark(dve.tensor_reduce(r[:, 0:1], pm[n % 2][:, 0:width], AX.X, ALU.max))
                if n in ADA_UNITS:
                    m = ADA_UNITS[n]
                    take_pair(m, 0, 2 * m, 0, src=pm[n % 2][:, TOK:TOK + 4])
                order.wait()
                if u["sink"] is None:
                    dve.tensor_scalar(r[:, 1:2], r[:, 0:1], unit_scale(u), -1.0, ALU.mult, ALU.mult).then_inc(
                        sem["shift_done"], 1)
                else:
                    dve.tensor_scalar(r[:, 1:2], r[:, 0:1], -ATTN_SCALE, col("sink", u["sink"]), ALU.mult, ALU.min).then_inc(
                        sem["shift_done"], 1)

            def normalise(n):
                u = UNITS[n]
                width = len(u["tiles"]) * P
                r = row[:, n % 8, :]
                dve.wait_ge(sem["exp_done"], n + 1)
                total = r[:, 2:3]
                if u["sink"] is not None:
                    dve.wait_ge(sem["exp_sink"], sum(x["sink"] is not None for x in UNITS[:n + 1]))
                    order.mark(dve.tensor_tensor(r[:, 5:6], r[:, 2:3], r[:, 3:4], ALU.add))
                    order.wait()
                    total = r[:, 5:6]
                order.mark(dve.reciprocal(r[:, 6:7], total))
                order.wait()
                dve.tensor_scalar(probs[:, n % 2, 0:width], probs[:, n % 2, 0:width], r[:, 6:7], None,
                                  ALU.mult).then_inc(sem["probs_done"], 1)

            for n in range(len(UNITS) + 1):
                if n < len(UNITS):
                    shift(n)
                if n >= 1:
                    if n >= 2:
                        copy_turned(n - 2)
                    normalise(n - 1)
                if n >= 3 and UNITS[n - 3]["last"]:
                    out_lo(UNITS[n - 3]["out"])
            copy_turned(len(UNITS) - 1)
            out_lo(len(OUTS) - 1)

            done = [0]

            def residual_phase(base, tokens, scale, norm=None, beside=None, per=0, pairs_from=None):
                first = done[0]
                if norm is not None:
                    order.mark(dve.memset(sum1[:, 0:tokens], 0.0))
                    order.wait()

                def evacuate(s, i, u, src):
                    n = 4 * i + u
                    dve.wait_ge(sem["psum_free"], s + 1)
                    dve.scalar_tensor_tensor(tile_of(n, tokens), tile_of(n, tokens), scale,
                                             tmp[:, u % 2, 0:tokens],
                                             ALU.mult, ALU.add).then_inc(sem["residual"], 1)
                    if norm is not None:
                        dve.wait_ge(sem["residual"], first + n + 1)
                        if not (norm == 0 and below(n, 1)):
                            dve.wait_ge(sem["added"], KT * norm + n)
                        dve.tensor_tensor(sum1[:, 0:tokens], sum1[:, 0:tokens], tile_of(n, tokens), ALU.add).then_inc(
                            sem["added"], 1)

                if base + KT == N_SLABS or pairs_from is not None:
                    for j in range(8):
                        step(base + j, 0, 0, lambda s, i, u, src, j=j: evacuate(s, 0, j, src),
                             first=norm is not None and j == 7)
                        if pairs_from is not None:
                            n = pairs_from + j // 2
                            if pairs_from == 20 and j in PAIR_AFTER:
                                take_pair(PAIR_AFTER[j], 0, 2 * PAIR_AFTER[j], PAIR_AFTER[j])
                            elif pairs_from > 20 and j % 2 == 1:
                                take_pair(n, 1, 2 * (n - 24), n)
                            n += 1
                            if j < 6 and j % 2 == (pairs_from == 20):
                                add_pair(n, (n // 2, n // 2 - 6)[n % 2], n % 2)
                else:
                    with dve.Fori(0, 2) as i:
                        order.enter(i, per)
                        for u in range(4):
                            step(base, i, u, evacuate, first=norm is not None and u == 3)
                            if beside is not None:
                                beside(i, u)
                        order.leave(2)
                done[0] += KT

            def fuse(c):
                g, b = col("ln_g", KT * c, KT), col("ln_b", KT * c, KT)
                layer, scale, shift_ = ((0, SC2, SH2), (1, SC1, SH1), (1, SC2, SH2))[c]
                dve.wait_ge(sem["ada_taken"], (20, 48, 48)[c])
                for k in range(2):
                    for out_, gain in ((0, g), (1, b)):
                        last = dve.scalar_tensor_tensor(fused[:, out_, :, k], mods[:, layer, scale:scale + KT, k], 1.0, gain,
                                                        ALU.add, ALU.mult)
                order.mark(last)
                order.wait()
                order.mark(dve.tensor_tensor(fused[:, 1, :, :], fused[:, 1, :, :],
                                             mods[:, layer, shift_:shift_ + KT, :], ALU.add))
                order.wait()

            def norm_phase(c, tokens):
                g, b = col("ln_g", KT * c, KT), col("ln_b", KT * c, KT)
                n = tokens // P
                dve.wait_ge(sem["stat_done"], c + 1)
                dve.tensor_copy(small[:, 0, 0:n], pm[2][:, 0:n]).then_inc(sem["mean_done"], 1)
                dve.wait_ge(sem["mean_done"], c + 1)
                order.mark(dve.tensor_tensor(small[:, 1, 0:n], small[:, 0, 0:n], small[:, 0, 0:n], ALU.mult))
                order.wait()
                dve.tensor_tensor(small[:, 1, 0:n], pm[2][:, 6:6 + n], small[:, 1, 0:n], ALU.subtract).then_inc(
                    sem["var_done"], 1)
                dve.wait_ge(sem["std2"], c + 1)
                dve.reciprocal(small[:, 2, 0:n], small[:, 2, 0:n]).then_inc(sem["r_done"], 1)
                dve.wait_ge(sem["spread"], 2 * c + 1)
                for n in range(KT + 2):
                    if n < KT:
                        dve.tensor_tensor(h_res[:, n, 0:tokens], h_res[:, n, 0:tokens], spread_m(0, tokens),
                                          ALU.subtract).then_inc(sem["less_mean"], 1)
                    if n == 2:
                        dve.wait_ge(sem["spread"], 2 * c + 2)
                    if n >= 2:
                        dve.wait_ge(sem["less_mean"], KT * c + n - 1)
                        dve.tensor_tensor(h_res[:, n - 2, 0:tokens], h_res[:, n - 2, 0:tokens], spread_r(0, tokens),
                                          ALU.mult).then_inc(sem["centred"], 1)
                if c == 3:
                    return
                for n in range(KT):
                    dve.wait_ge(sem["mod_f"], KT * (c + 1) + n + 1)
                    dve.wait_ge(sem["centred"], KT * c + n + 1)
                    dve.tensor_scalar(h_res[:, n, 0:tokens], h_res[:, n, 0:tokens], g[:, n:n + 1], b[:, n:n + 1],
                                      ALU.mult, ALU.add).then_inc(sem["h_ready"], 1)
                dve.wait_ge(sem["h_ready"], KT * (c + 1))

            fuse(0)
            residual_phase(S_ATTN_OUT, TOK, ALPHA, norm=0, pairs_from=20)
            add_pair(24, 12, 0)
            norm_phase(0, TOK)

            def ffn(base, layer, tokens):
                s0 = base
                done = FT * layer
                for g, tiles in enumerate(FF_GROUPS):
                    def beside(i, u):
                        m = (s0 - S_FFN0) // 2 + u // 2 + 2 * i
                        if layer == 0 and g < 2 and u % 2 == 0:
                            add_pair(25 + m, (6, 13)[u // 2] + (s0 - S_FFN0) // 4 + i, 1 - u // 2)
                        if layer == 0 and g < 2 and u % 2 == 1:
                            take_pair(24 + m, 1, 2 * m, u // 2)

                    per = 2 * (KT - 1) if layer == 0 and g < 2 else 0

                    with dve.Fori(0, tiles // 2) as i:
                        order.enter(i, 4 + per)
                        for u in range(4):
                            def evacuate(s, i, u, src):
                                j = sum(FF_GROUPS[:g]) + 2 * i + u // 2
                                tile = j + FT * (u % 2)
                                pair = done + 2 * i + u // 2
                                acc = (acc_g, acc_v)[u % 2]
                                before = vec[:, bass.ds(VEC["conv_w"] + 2 * FT * (CONV_W * layer) + tile, 1)]
                                after = vec[:, bass.ds(VEC["conv_w"] + 2 * FT * (CONV_W * layer + 2) + tile, 1)]
                                dve.wait_ge(sem["lin_done"], 2 * pair + u % 2 + 1)
                                halves = HALVES if tokens == TOK else HALVES[:1]
                                for a, b in halves:
                                    last = dve.scalar_tensor_tensor(acc[:, a + 1:b], src[:, a:b - 1], before, acc[:, a + 1:b],
                                                                    ALU.mult, ALU.add)
                                order.mark(last)
                                order.wait()
                                for a, b in halves:
                                    last = dve.scalar_tensor_tensor(acc[:, a:b - 1], src[:, a + 1:b], after, acc[:, a:b - 1],
                                                                    ALU.mult, ALU.add)
                                last.then_inc(sem["psum_free"], 1)
                                if u % 2 == 1:
                                    dve.wait_ge(sem["psum_free"], s + 1)
                                    dve.wait_ge(sem["silu_done"], pair + 1)
                                    dve.tensor_tensor(hid_f[:, 0:tokens], acc_g[:, 0:tokens], acc_v[:, 0:tokens],
                                                      ALU.mult).then_inc(sem["acc_free"], 1)
                                    dve.wait_ge(sem["hid_split"], pair + 1)
                                    dve.tensor_tensor(hid_lo[:, bass.ds(2 * i + u // 2, 1), 0:tokens].rearrange("p a b -> p (a b)"),
                                                      hid_f[:, 0:tokens],
                                                      hid_hi[:, bass.ds(2 * i + u // 2, 1), 0:tokens].rearrange("p a b -> p (a b)").bitcast(FP32),
                                                      ALU.subtract).then_inc(sem["hid_ready"], 1)
                            step(s0, i, u, evacuate)
                            beside(i, u)
                        order.leave(tiles // 2)
                    done += tiles
                    s0 += 2 * tiles
                    if layer == 0 and g == 2:
                        fuse(1)
                    residual_phase(s0, tokens, ALPHA if g == 0 else 1.0, norm=None if g < 2 else 1 + 2 * layer,
                                   beside=beside, per=per, pairs_from=44 if layer == 0 and g == 1 else None)
                    s0 += KT

            ffn(S_FFN0, 0, TOK)
            norm_phase(1, TOK)

            order.mark(dve.memset(restart[:, :], 1.0))
            order.wait()
            order.mark(dve.memset(chunks(restart[:, :])[:, :, 0:1], 0.0))

            def decays(j):
                z, h = j // GLA_HEADS, j % GLA_HEADS
                dve.wait_ge(sem["abs_done"], j + 1)
                if j >= 1:
                    dve.wait_ge(sem["ld_done"], j)
                order.mark(dve.tensor_scalar(clipped[:, :], pm[2 + j % 2][:, 0:TOK], col("b_a", j), 0.0, ALU.add, ALU.min))
                order.wait()
                dve.wait_ge(sem["log_done"], j + 1)
                order.mark(dve.tensor_tensor(clipped[:, :], clipped[:, :], soft[:, j % 2, :], ALU.subtract))
                order.wait()
                order.mark(dve.tensor_tensor_scan(cum[:, z, h, :], restart[:, :], clipped[:, :], 0.0, ALU.mult, ALU.add))
                order.wait()
                last = dve.tensor_copy(chunk_sum[:, z, h, :].unsqueeze(2), chunks(cum[:, z, h, :])[:, :, P - 1:P])
                if z == 1:
                    order.mark(last)
                    order.wait()
                    last = dve.tensor_tensor(cum[:, z, h, :], cum[:, z, h, :], clipped[:, :], ALU.subtract)
                last.then_inc(sem["ld_done"], 1)

            step(S_GLA, 0, 0)
            for n in range(GLA_HEADS):
                step(S_GLA, 0, n + 1)
                decays(2 * n)
                decays(2 * n + 1)
            with dve.Fori(0, 2) as i:
                for u in range(4):
                    step(S_GLA + 1 + GLA_HEADS, i, u)
            with dve.Fori(0, 3) as i:
                for u in range(4):
                    step(S_GLA + N_GLA_ALL, i, u)

            dve.wait_ge(sem["psum_free"], S_GLA_OUT)
            dve.wait_ge(sem["v_copied"], TOK // P + 8)
            dve.wait_ge(sem["decay_done"], 1)
            dve.wait_ge(sem["level_in"], 16)
            dve.tensor_copy(level[:, :, :], level_f[:, :, :]).then_inc(sem["level_done"], 1)
            dve.wait_ge(sem["level_done"], 1)

            def totals(z, h, n):
                return chunk_sum[:, z, h, 0:n].unsqueeze(2).to_broadcast([P, n, P])

            def level_diff(m):
                if m >= GLA_HEADS * (LEVELS - 1):
                    return
                h, lv = m // (LEVELS - 1), m % (LEVELS - 1)
                if m >= 4:
                    dve.wait_ge(sem["both_done"], m - 3)
                left, right, mid = segments(lv // 2, lv % 2, h)
                to_left, to_right, _ = segments(lv // 2, lv % 2, h, fade[:, m % 4, :])
                dve.tensor_tensor(to_left, mid, left, ALU.subtract)
                dve.tensor_tensor(to_right, right, mid, ALU.subtract).then_inc(sem["diff_done"], 1)

            def key_diff(h):
                if h >= 1:
                    dve.wait_ge(sem["k_turned"], 2 * h)
                dve.tensor_tensor(chunks(k_out[:, :]), totals(0, h, 6), chunks(cum[:, 0, h, :]), ALU.subtract).then_inc(
                    sem["k_diff"], 1)

            def scan(q):
                h, z = q // 2, q % 2
                dve.wait_ge(sem["s_prod"], q + 1)
                if h >= 1:
                    dve.wait_ge(sem["o_done"], h)
                for j in range(5):
                    n = 5 * q + j
                    dst, src = state(z, STATE[z][j]), state_sum(j)
                    if j == 0:
                        dve.tensor_copy(dst, src).then_inc(sem["s_done"], 1)
                    else:
                        dve.wait_ge(sem["s_done"], n)
                        c = SCAN[z][j]
                        dve.scalar_tensor_tensor(dst, state(z, STATE[z][j - 1]), decay[:, z, h, c:c + 1], src,
                                                 ALU.mult, ALU.add).then_inc(sem["s_done"], 1)

            def query_diff(h):
                if h >= 1:
                    dve.wait_ge(sem["o_done"], h)
                dve.tensor_tensor(chunks(q_in[:, 1, :]), totals(1, h, 4), chunks(cum[:, 1, h, 0:LAT]), ALU.subtract).then_inc(
                    sem["q_diff"], 1)

            def output_rms(h):
                dve.wait_ge(sem["o_std"], h + 1)
                dve.reciprocal(small[:, 3, 0:4], small[:, 2, 0:4]).then_inc(sem["o_rms"], 1)

            def scale_output(h):
                dve.wait_ge(sem["o_r_copied"], h + 1)
                for vt in range(2):
                    dve.scalar_tensor_tensor(o_buf[:, vt, :], pm[3][:, 512 * vt:512 * (vt + 1)], col("head_norm", vt),
                                             o_r[:, :], ALU.mult, ALU.mult).then_inc(sem["o_scaled"], 1)

            def output_low(h):
                for vt in range(2):
                    dve.wait_ge(sem["o_hi_done"], 2 * h + vt + 1)
                    dve.tensor_tensor(o_lo2[:, 2 * h + vt, :], o_buf[:, vt, :], o_hi2[:, 2 * h + vt, :].bitcast(FP32),
                                      ALU.subtract).then_inc(sem["o_ready"], 1)

            key_diff(0)
            for m in range(3):
                level_diff(m)
            for h in range(GLA_HEADS):
                for lv in range(LEVELS - 1):
                    level_diff((LEVELS - 1) * h + lv + 3)
                    n = LEVELS * h + lv + 1
                    dve.wait_ge(sem["gram_done"], n + 1)
                    dve.wait_ge(sem["level_used"], n)
                    dve.copy_predicated(chunks(pairs[:, h % 2, :]), level[:, lv, :].unsqueeze(1).to_broadcast([P, 4, P]),
                                        chunks(level_bank(n))).then_inc(sem["level_used"], 1)
                    if h >= 1 and lv == 7:
                        output_rms(h - 1)
                    if h >= 1 and lv == 9:
                        scale_output(h - 1)
                    if lv == 8:
                        query_diff(h)
                    if lv == 11:
                        scan(2 * h)
                    if lv == 12 and h + 1 < GLA_HEADS:
                        key_diff(h + 1)
                scan(2 * h + 1)
                if h >= 1:
                    output_low(h - 1)
            output_rms(GLA_HEADS - 1)
            scale_output(GLA_HEADS - 1)
            output_low(GLA_HEADS - 1)

            fuse(2)
            residual_phase(S_GLA_OUT, LAT, ALPHA, norm=2)
            norm_phase(2, LAT)
            ffn(S_FFN1, 1, LAT)
            norm_phase(3, LAT)

        @block.gpsimd
        def _(pool):
            order = Order(pool, sem["pool_seq"])

            def low_part(first, tokens):
                for n in range(KT):
                    pool.wait_ge(sem["x_hi_done"], first + n + 1)
                    pool.tensor_tensor(x_lo[:, n, 0:tokens], mod_t[:, n % 4, 0:tokens], x_hi[:, n, 0:tokens].bitcast(FP32),
                                       ALU.subtract).then_inc(sem["x_ready"], 1)

            low_part(0, TOK)

            def add_up(products, weights, c, slot):
                def tiles(a, b):
                    return products[:, :, a * P:b * P]

                order.mark(pool.tensor_tensor(products[:, :, :].rearrange("p a (k f) -> p a k f", f=P),
                                              weights[:, :, :].rearrange("p a (k f) -> p a k f", f=P),
                                              cond[:, :, c].unsqueeze(1).unsqueeze(3).to_broadcast([P, 2, KT, P]), ALU.mult))
                order.wait()
                order.mark(pool.tensor_tensor(tiles(0, 4), tiles(0, 4), tiles(4, 8), ALU.add))
                order.wait()
                order.mark(pool.tensor_tensor(tiles(0, 2), tiles(0, 2), tiles(2, 4), ALU.add))
                order.wait()
                return pool.tensor_tensor(ada_sum[:, slot, c, :].rearrange("p (a b) -> p a b", a=2),
                                          tiles(0, 1), tiles(1, 2), ALU.add)

            def add_pair(n, count, buffer):
                pair_arrived(pool, n, count, buffer)
                pool.wait_ge(sem["ada_sum_lat"], n - 7)
                add_up(ada_w[buffer], ada_w[buffer], 1, buffer).then_inc(sem["ada_sum_ctx"], 1)

            for s in range(N_ATTN_IN):
                if s < 6:
                    pool.wait_ge(sem["psum_free"], s + 1)
                    if s >= 4:
                        pool.wait_ge(sem["ssq_done"], s - 3)
                    pool.tensor_tensor(square(s), qkv[:, s, :], qkv[:, s, :], ALU.mult).then_inc(sem["squared"], 1)
                if 3 <= s <= 13 and s % 2 == 1:
                    add_pair(8 + (s - 3) // 2, (s - 3) // 4 + 1, (s - 3) // 2 % 2)

            def sums_phase(c, tokens):
                order.mark(pool.memset(sum2[:, 0:tokens], 0.0))
                order.wait()
                for n in range(KT):
                    if c == 0 and n % 2 == 0 and n > 0:
                        add_pair(20 + n // 2, (10, 4, 11, 5)[n // 2], n // 2 % 2)
                    pool.wait_ge(sem["squared_h"], KT * c + n + 1)
                    if n >= 1:
                        pool.wait_ge(sem["summed"], KT * c + n)
                    pool.tensor_tensor(sum2[:, 0:tokens], sum2[:, 0:tokens], sq_t[:, n % 2, 0:tokens],
                                       ALU.add).then_inc(sem["summed"], 1)

            for n in range(14, 21):
                pair_arrived(pool, n, n - 10, 0)
                if n == 14:
                    pool.wait_ge(sem["ada_sum_lat"], 6)
                pool.wait_ge(sem["ada_sum_ctx"], n - 8)
                order.mark(add_up(ada_w[1], ada_w[0], 0, n % 2))
                order.wait()
                pool.sem_inc(sem["ada_sum_lat"], 1)
                add_up(ada_w[0], ada_w[0], 1, n % 2).then_inc(sem["ada_sum_ctx"], 1)

            pool.wait_ge(sem["pv_copied"], len(OUTS))
            sums_phase(0, TOK)
            add_pair(24, 12, 0)
            low_part(KT, TOK)
            add_pair(25, 6, 1)
            with pool.Fori(0, 11) as i:
                order.enter(i, 6)
                for u in range(2):
                    add_pair(26 + 2 * i + u, (13, 7)[u] + i, u)
                order.leave(11)
            sums_phase(1, TOK)
            low_part(2 * KT, TOK)

            pool.wait_ge(sem["psum_free"], S_GLA_OUT)

            def fade_keys(q):
                pool.wait_ge(sem["k_exp"], q + 1)
                pool.tensor_tensor(k_out[:, :], k_out[:, :], gla_k[:, q // 2, :], ALU.mult).then_inc(sem["k_done"], 1)

            def fade_queries(h):
                pool.wait_ge(sem["q_exp"], h + 1)
                for z in range(2):
                    last = pool.tensor_tensor(q_in[:, z, :], q_in[:, z, :], gla_q[:, h, :], ALU.mult)
                last.then_inc(sem["q_done"], 1)

            def gate_output(h):
                for vt in range(2):
                    pool.wait_ge(sem["o_scaled"], 2 * h + vt + 1)
                    pool.tensor_tensor(o_buf[:, vt, :], o_buf[:, vt, :], gla_g[:, 2 * h + vt, :], ALU.mult).then_inc(
                        sem["o_gated"], 1)

            fade_keys(0)
            for h in range(GLA_HEADS):
                for lv in range(LEVELS - 1):
                    b, z = lv // 2, lv % 2
                    m = (LEVELS - 1) * h + lv
                    pool.wait_ge(sem["fade_done"], m + 1)
                    if m >= 3:
                        pool.wait_ge(sem["gram_done"], LEVELS * ((m - 3) // (LEVELS - 1)) + (m - 3) % (LEVELS - 1) + 2)
                    sides = (gla_k, gla_q) if z == 0 else (gla_q, gla_k)
                    for side in range(2):
                        last = pool.tensor_tensor(segments(b, z, h, both(m))[side],
                                                  segments(b, z, h, fade[:, m % 4, :])[side],
                                                  segments(b, z, h, sides[side][:, h, 0:LAT])[side], ALU.mult)
                    last.then_inc(sem["both_done"], 1)
                    if lv == 8:
                        fade_keys(2 * h + 1)
                    if h >= 1 and lv == 10:
                        gate_output(h - 1)
                    if lv == 12:
                        fade_queries(h)
                if h + 1 < GLA_HEADS:
                    fade_keys(2 * h + 2)
            gate_output(GLA_HEADS - 1)

            pool.wait_ge(sem["o_ready"], KT)
            sums_phase(2, LAT)
            low_part(3 * KT, LAT)
            sums_phase(3, LAT)


UNITS, OUTS = [], []


def _units():
    heads = [("b", h) for h in range(N_HEADS)] + [("a", h) for h in range(N_HEADS)]
    for group, h in heads:
        kv = h // (N_HEADS // N_KV)
        for first, last, tokens in ((0, LAT, "lat"), (LAT, TOK, "ctx")):
            blocks = list(range(first, last, P))
            for q0 in blocks:
                band = None
                if tokens == "ctx":
                    keys = [(LAT, TOK)]
                elif group == "a":
                    keys = [(0, LAT), (LAT, TOK)]
                else:
                    lo, hi = max(q0 - P, 0), min(q0 + 2 * P, LAT)
                    keys = [(lo, hi), (LAT, TOK)]
                    band = ([(0, 0)] if lo < q0 else []) + ([(hi - P - lo, 2 * P)] if hi > q0 + P else [])
                spans, at = [], 0
                for a, b in keys:
                    while a < b:
                        n = min(b - a, 512 - at % 512)
                        spans.append((at, a, a + n))
                        at, a = at + n, a + n
                tiles = [t for a, b in keys for t in range(a // P, b // P)]
                UNITS.append(dict(q=HEAD_OF[group + "q"] + h, k=HEAD_OF[group + "k"] + kv,
                                  v=kv + (N_KV if group == "b" else 0), q0=q0, spans=spans, tiles=tiles, band=band,
                                  sink=h if group == "b" else None, out=len(OUTS), o0=q0 - first,
                                  first=q0 == first, last=q0 == blocks[-1]))
            OUTS.append((h + (N_HEADS if group == "b" else 0), first, last))


_units()
ADA_UNITS = {8 + 7 * j: 14 + j for j in range(6)}
PAIR_AFTER = {2: 20, 4: 21, 6: 22, 7: 23}
UNITS_B = sum(u["sink"] is not None for u in UNITS)


def _slabs(attn_w_in, attn_w_out, gla_w_in, gla_w_a1, gla_w_out, ffn_w_up, ffn_w_down):
    import numpy as np

    def cut(w, n, rows=None):
        w = w[:, n * P:(n + 1) * P] if rows is None else w[rows[0] * P:rows[1] * P, n * P:(n + 1) * P]
        full = np.zeros((KT * P, P), w.dtype)
        full[:w.shape[0], :w.shape[1]] = w
        return full.reshape(KT, P, P).transpose(1, 0, 2).reshape(P, KT * P)

    def ffn(layer):
        got, first = [], 0
        for tiles in FF_GROUPS:
            for j in range(first, first + tiles):
                got += [cut(ffn_w_up[layer], j), cut(ffn_w_up[layer], FT + j)]
            got += [cut(ffn_w_down[layer], n, (first, first + tiles)) for n in range(KT)]
            first += tiles
        return got

    got = [cut(attn_w_in[0], n) for n in ATTN_COLS] + [cut(attn_w_out[0], n) for n in range(KT)] + ffn(0)
    rank = np.concatenate([gla_w_a1[0, 0], gla_w_a1[0, 1]], axis=1)
    got += [cut(rank, 0)] + [cut(gla_w_in[0], n) for n in (*range(4, 16), *range(0, 4), *range(16, 24))]
    got += [cut(gla_w_out[0], n) for n in range(KT)] + ffn(1)
    return np.stack(got)


def _columns(a):
    return a.reshape(-1, P).T


def kernel(x, c, ctx, c_ctx, ada_w, ada_b, ln_g, ln_b, ffn_w_up, ffn_conv_w, ffn_conv_b, ffn_w_down,
           attn_w_in, attn_q_norm, attn_k_norm, attn_sink, attn_w_out,
           gla_w_in, gla_w_a1, gla_w_a2, gla_b_a, gla_head_norm, gla_w_out):
    import numpy as np
    import concourse.bacc as bacc
    from concourse.bass_utils import run_bass_kernel_spmd

    arrays = _arrays(np, x, c, ctx, c_ctx, ada_w, ada_b, ln_g, ln_b, ffn_w_up, ffn_conv_w, ffn_conv_b, ffn_w_down,
                     attn_w_in, attn_q_norm, attn_k_norm, attn_sink, attn_w_out,
                     gla_w_in, gla_w_a1, gla_w_a2, gla_b_a, gla_head_norm, gla_w_out)
    nc = bacc.Bacc("TRN2", target_bir_lowering=False, num_devices=1)
    build(nc, arrays)
    got = run_bass_kernel_spmd(nc, [arrays], core_ids=[0]).results[0]["out"]
    return np.ascontiguousarray(np.asarray(got).transpose(2, 1, 0).reshape(1, LAT, D_MODEL))


def build(nc, arrays):
    args = [nc.dram_tensor(n, a.shape, mybir.dt.from_np(a.dtype), kind="ExternalInput").ap() for n, a in arrays.items()]
    args.append(nc.dram_tensor("out", [P, KT, LAT], FP32, kind="ExternalOutput").ap())
    trunk(nc, *args)


def _arrays(np, x, c, ctx, c_ctx, ada_w, ada_b, ln_g, ln_b, ffn_w_up, ffn_conv_w, ffn_conv_b, ffn_w_down,
            attn_w_in, attn_q_norm, attn_k_norm, attn_sink, attn_w_out,
            gla_w_in, gla_w_a1, gla_w_a2, gla_b_a, gla_head_norm, gla_w_out):
    tokens = np.concatenate([x[0], ctx[0]], axis=0)
    cond = np.stack([_columns(c[0]), _columns(c_ctx)], axis=-1).reshape(P, 2 * KT)
    vec = np.concatenate([
        cond, _columns(ada_b), _columns(ln_g), _columns(ln_b), _columns(ffn_conv_w), _columns(ffn_conv_b),
        _columns(attn_q_norm), _columns(attn_k_norm), np.broadcast_to(attn_sink, (P, N_HEADS)),
        _columns(gla_b_a), _columns(gla_head_norm), np.full((P, 1), EPS, np.float32)], axis=1)
    ada = ada_w.reshape(2, KT, P, ADA_TILES // 2, 2, P).transpose(0, 3, 2, 4, 1, 5).reshape(ADA_TILES, P, 2 * KT * P)
    a2 = np.zeros((2 * GLA_RANK, 2, GLA_HEADS * P), np.float32)
    for z in range(2):
        a2[z * GLA_RANK:(z + 1) * GLA_RANK, z] = gla_w_a2[0, z]

    t = np.arange(LAT)
    freq = np.power(np.float32(ROPE_THETA), -np.arange(HEAD_DIM // 4, dtype=np.float32) * 2.0 / (HEAD_DIM // 2))
    freq = freq.astype(np.float32)
    angle = np.concatenate([(t // GRID_W).astype(np.float32)[:, None] * freq,
                            (t % GRID_W).astype(np.float32)[:, None] * freq], axis=-1).T
    rope = np.stack([np.concatenate([np.cos(angle)] * 2), np.concatenate([np.sin(angle), -np.sin(angle)])], axis=1)
    q, k = np.arange(P)[:, None], np.arange(3 * P)[None, :] - P
    band = np.where(np.abs(k - q) <= WINDOW, 0.0, MASKED)
    first, second = np.arange(P)[:, None], np.arange(P)[None, :]
    level = []
    for b in range(GLA_LEVELS):
        m = 1 << b
        pair = (first // (2 * m) == second // (2 * m)) & (first // m != second // m)
        level += [pair & (first < second), pair & (first > second)]
    out = {
        "x": tokens.T.reshape(KT, P, TOK).transpose(1, 0, 2), "vec": vec,
        "slabs": _slabs(attn_w_in, attn_w_out, gla_w_in, gla_w_a1, gla_w_out, ffn_w_up, ffn_w_down),
        "ada": ada, "rope": rope, "band": band, "eye": np.eye(P), "a2": a2,
        "level": np.stack(level, axis=1)}
    return {n: np.ascontiguousarray(a, dtype=np.float32) for n, a in out.items()}
```
